# Optimizing a Trainium2 kernel written in Bass

```python
import math
import jax
import jax.numpy as jnp
from jax import lax

D_MODEL = 1024
BATCH = 1
SEQ = 256
DEPTH = 2

GRID_W = 64
CTX_LEN = 256
HEAD_DIM = 64
A_HEADS = 4
B_HEADS = 8
B_KV = 2
C_HEADS = 8
C_KV = 2
WINDOW = 128
QBLK = 128
D_FF = 4 * D_MODEL
ROPE_THETA = 10000.0
EPS = 1e-6
SUBLN_EPS = 1e-5

A_W = A_HEADS * 2 * HEAD_DIM
B_W = B_HEADS * HEAD_DIM
C_W = C_HEADS * HEAD_DIM
MIX_W = A_W + B_W + C_W
B_KW = B_KV * HEAD_DIM
C_KW = C_KV * HEAD_DIM
IN_SIZES = (A_W, A_W, A_W, B_W, B_KW, B_KW, C_W, C_KW, C_KW, 3 * D_MODEL)
IN_SPLITS = tuple(sum(IN_SIZES[:i + 1]) for i in range(len(IN_SIZES) - 1))
IN_W = sum(IN_SIZES)

kernel_name = 'hybrid_diffusion_trunk'

def rms_norm(x, gain, eps=EPS):
    x32 = x.astype(jnp.float32)
    y = x32 * lax.rsqrt(jnp.mean(jnp.square(x32), axis=-1, keepdims=True) + eps)
    return (y * gain.astype(jnp.float32)).astype(x.dtype)

def modulate(x, gain, shift, scale):
    return rms_norm(x, gain) * (1 + scale) + shift

def axial_tables(rows):
    row = jnp.repeat(jnp.arange(rows, dtype=jnp.int32), GRID_W).astype(jnp.float32)
    col = jnp.tile(jnp.arange(GRID_W, dtype=jnp.int32), rows).astype(jnp.float32)
    half = HEAD_DIM // 2
    inv_freq = jnp.power(ROPE_THETA, -jnp.arange(0, half, 2, dtype=jnp.float32) / half)
    ang_r = row[:, None] * inv_freq[None, :]
    ang_c = col[:, None] * inv_freq[None, :]
    return (jnp.cos(ang_r)[None, :, None, :], jnp.sin(ang_r)[None, :, None, :],
            jnp.cos(ang_c)[None, :, None, :], jnp.sin(ang_c)[None, :, None, :])

def _rot(x, cos, sin):
    x1, x2 = jnp.split(x, 2, axis=-1)
    return jnp.concatenate([x1 * cos - x2 * sin, x2 * cos + x1 * sin], axis=-1)

def rope_2d(x, tabs):
    cos_r, sin_r, cos_c, sin_c = tabs
    xr, xc = jnp.split(x.astype(jnp.float32), 2, axis=-1)
    return jnp.concatenate([_rot(xr, cos_r, sin_r), _rot(xc, cos_c, sin_c)], axis=-1).astype(x.dtype)

def rope_pairs(x, tabs):
    b, n, h, m, d = x.shape
    return rope_2d(x.reshape(b, n, h * m, d), tabs).reshape(b, n, h, m, d)

def split_proj(p):
    b, n, _ = p.shape
    qa, ka, va, qb, kb, vb, qc, kc, vc, gt = jnp.split(p, IN_SPLITS, axis=-1)
    return (qa.reshape(b, n, A_HEADS, 2, HEAD_DIM), ka.reshape(b, n, A_HEADS, 2, HEAD_DIM),
            va.reshape(b, n, A_HEADS, 2 * HEAD_DIM),
            qb.reshape(b, n, B_HEADS, HEAD_DIM), kb.reshape(b, n, B_KV, HEAD_DIM), vb.reshape(b, n, B_KV, HEAD_DIM),
            qc.reshape(b, n, C_HEADS, HEAD_DIM), kc.reshape(b, n, C_KV, HEAD_DIM), vc.reshape(b, n, C_KV, HEAD_DIM),
            gt)

def gqa_attend(q, k, v, sink=None):
    b, sq, h, d = q.shape
    kvh = k.shape[2]
    g = h // kvh
    nblk = sq // QBLK
    scale = d ** -0.5
    qb = q.reshape(b, nblk, QBLK, kvh, g, d).transpose(1, 0, 2, 3, 4, 5)

    def block(qi):
        s = jnp.einsum('bqngd,bknd->bngqk', qi, k, preferred_element_type=jnp.float32) * scale
        if sink is None:
            p = jax.nn.softmax(s, axis=-1)
        else:
            sk = sink.astype(jnp.float32).reshape(1, kvh, g, 1, 1)
            m = jnp.maximum(jnp.max(s, axis=-1, keepdims=True), sk)
            e = jnp.exp(s - m)
            p = e / (jnp.sum(e, axis=-1, keepdims=True) + jnp.exp(sk - m))
        return jnp.einsum('bngqk,bkne->bqnge', p.astype(v.dtype), v)

    o = lax.map(block, qb)
    return o.transpose(1, 0, 2, 3, 4, 5).reshape(b, sq, h, v.shape[-1])

def diff_attend(q, k, v, lam):
    b, sq, h, _, d = q.shape
    nblk = sq // QBLK
    scale = d ** -0.5
    qb = q.reshape(b, nblk, QBLK, h, 2, d).transpose(1, 0, 2, 3, 4, 5)

    def block(qi):
        s = jnp.einsum('bqhmd,bkhmd->bhmqk', qi, k, preferred_element_type=jnp.float32) * scale
        p = jax.nn.softmax(s, axis=-1)
        pd = p[:, :, 0] - lam * p[:, :, 1]
        return jnp.einsum('bhqk,bkhe->bqhe', pd.astype(v.dtype), v)

    o = lax.map(block, qb)
    return o.transpose(1, 0, 2, 3, 4).reshape(b, sq, h, v.shape[-1])

def window_attend(q, k, v, kc, vc, sink):
    b, s, h, d = q.shape
    kvh = k.shape[2]
    g = h // kvh
    nblk = s // QBLK
    scale = d ** -0.5

    def band(t):
        tp = jnp.pad(t, ((0, 0), (QBLK, QBLK), (0, 0), (0, 0))).reshape(b, nblk + 2, QBLK, kvh, t.shape[-1])
        return jnp.concatenate([tp[:, :-2], tp[:, 1:-1], tp[:, 2:]], axis=2)

    kband, vband = band(k), band(v)
    qb = q.reshape(b, nblk, QBLK, kvh, g, d)
    s_loc = jnp.einsum('bjqngd,bjknd->bjngqk', qb, kband, preferred_element_type=jnp.float32) * scale
    s_ctx = jnp.einsum('bjqngd,bknd->bjngqk', qb, kc, preferred_element_type=jnp.float32) * scale
    blk = jnp.arange(nblk, dtype=jnp.int32)[:, None, None]
    qpos = blk * QBLK + jnp.arange(QBLK, dtype=jnp.int32)[None, :, None]
    kpos = (blk - 1) * QBLK + jnp.arange(3 * QBLK, dtype=jnp.int32)[None, None, :]
    valid = (jnp.abs(kpos - qpos) <= WINDOW) & (kpos >= 0) & (kpos < s)
    s_loc = jnp.where(valid[None, :, None, None], s_loc, -jnp.inf)
    sk = sink.astype(jnp.float32).reshape(1, 1, kvh, g, 1, 1)
    m = jnp.maximum(jnp.maximum(jnp.max(s_loc, axis=-1, keepdims=True), jnp.max(s_ctx, axis=-1, keepdims=True)), sk)
    e_loc = jnp.exp(s_loc - m)
    e_ctx = jnp.exp(s_ctx - m)
    denom = jnp.sum(e_loc, axis=-1, keepdims=True) + jnp.sum(e_ctx, axis=-1, keepdims=True) + jnp.exp(sk - m)
    o = (jnp.einsum('bjngqk,bjkne->bjqnge', (e_loc / denom).astype(v.dtype), vband)
         + jnp.einsum('bjngqk,bkne->bjqnge', (e_ctx / denom).astype(v.dtype), vc))
    return o.reshape(b, s, h, v.shape[-1])

def diff_post(o, g_subln, lam_init):
    b, n = o.shape[:2]
    return (rms_norm(o, g_subln, SUBLN_EPS) * (1.0 - lam_init)).reshape(b, n, A_W)

def flat_heads(o):
    b, n = o.shape[:2]
    return o.reshape(b, n, -1)

def merge_branches(oa, ob, oc, gt, w_branch, w_out):
    ga, gb, gc = jnp.split(jax.nn.sigmoid(gt), 3, axis=-1)
    z = (ga * (oa @ w_branch[:A_W]) + gb * (ob @ w_branch[A_W:A_W + B_W])
         + gc * (oc @ w_branch[A_W + B_W:]))
    return z @ w_out

def sq_relu_mlp(h, w1, w2):
    return jnp.square(jax.nn.relu(h @ w1)) @ w2

def setup_inputs(seed: int = 0) -> dict:
    key = jax.random.key(seed)
    ks = jax.random.split(key, 24)
    f32 = jnp.float32
    L = DEPTH

    def nrm(k, shape, scale):
        return jax.random.normal(k, shape, f32) * scale

    return {
        'x': nrm(ks[0], (BATCH, SEQ, D_MODEL), 1.0),
        'c': nrm(ks[1], (BATCH, D_MODEL), 1.0),
        'ctx': nrm(ks[2], (BATCH, CTX_LEN, D_MODEL), 1.0),
        'c_ctx': nrm(ks[3], (D_MODEL,), 1.0),
        'w_ada': nrm(ks[4], (L, D_MODEL, 6 * D_MODEL), 0.5 * D_MODEL ** -0.5),
        'b_ada': nrm(ks[5], (L, 6 * D_MODEL), 0.01),
        'g_pre_mix': 1.0 + nrm(ks[6], (L, D_MODEL), 0.02),
        'g_post_mix': 1.0 + nrm(ks[7], (L, D_MODEL), 0.02),
        'g_pre_ff': 1.0 + nrm(ks[8], (L, D_MODEL), 0.02),
        'g_post_ff': 1.0 + nrm(ks[9], (L, D_MODEL), 0.02),
        'w_in': nrm(ks[10], (L, D_MODEL, IN_W), D_MODEL ** -0.5),
        'g_qnorm': 1.0 + nrm(ks[11], (L, HEAD_DIM), 0.02),
        'g_knorm': 1.0 + nrm(ks[12], (L, HEAD_DIM), 0.02),
        'lam_q1': nrm(ks[13], (L, HEAD_DIM), 0.1),
        'lam_k1': nrm(ks[14], (L, HEAD_DIM), 0.1),
        'lam_q2': nrm(ks[15], (L, HEAD_DIM), 0.1),
        'lam_k2': nrm(ks[16], (L, HEAD_DIM), 0.1),
        'g_subln': 1.0 + nrm(ks[17], (L, 2 * HEAD_DIM), 0.02),
        'sink': nrm(ks[18], (L, C_HEADS), 0.5),
        'w_branch': nrm(ks[19], (L, MIX_W, D_MODEL), A_W ** -0.5),
        'w_out': nrm(ks[20], (L, D_MODEL, D_MODEL), D_MODEL ** -0.5),
        'w_ff1': nrm(ks[21], (L, D_MODEL, D_FF), D_MODEL ** -0.5),
        'w_ff2': nrm(ks[22], (L, D_FF, D_MODEL), D_FF ** -0.5),
    }

def reference(x, c, ctx, c_ctx, w_ada, b_ada, g_pre_mix, g_post_mix, g_pre_ff, g_post_ff, w_in, g_qnorm, g_knorm,
              lam_q1, lam_k1, lam_q2, lam_k2, g_subln, sink, w_branch, w_out, w_ff1, w_ff2):
    n_tok = x.shape[1]
    rows = n_tok // GRID_W
    tabs = axial_tables(rows)
    y = ctx
    silu_c = jax.nn.silu(c)
    silu_cc = jax.nn.silu(c_ctx)
    for l in range(DEPTH):
        lam_init = 0.8 - 0.6 * math.exp(-0.3 * l)
        lam = (jnp.exp(jnp.sum(lam_q1[l].astype(jnp.float32) * lam_k1[l].astype(jnp.float32)))
               - jnp.exp(jnp.sum(lam_q2[l].astype(jnp.float32) * lam_k2[l].astype(jnp.float32))) + lam_init)
        sh1, sc1, gm1, sh2, sc2, gm2 = jnp.split((silu_c @ w_ada[l] + b_ada[l])[:, None, :], 6, axis=-1)
        csh1, csc1, cgm1, csh2, csc2, cgm2 = jnp.split((silu_cc @ w_ada[l] + b_ada[l])[None, None, :], 6, axis=-1)

        qa_x, ka_x, va_x, qb_x, kb_x, vb_x, qc_x, kc_x, vc_x, gt_x = split_proj(
            modulate(x, g_pre_mix[l], sh1, sc1) @ w_in[l])
        qa_y, ka_y, va_y, qb_y, kb_y, vb_y, qc_y, kc_y, vc_y, gt_y = split_proj(
            modulate(y, g_pre_mix[l], csh1, csc1) @ w_in[l])
        qa_x = rope_pairs(qa_x, tabs)
        ka_x = rope_pairs(ka_x, tabs)
        qb_x = rope_2d(rms_norm(qb_x, g_qnorm[l]), tabs)
        kb_x = rope_2d(rms_norm(kb_x, g_knorm[l]), tabs)
        kb_y = rms_norm(kb_y, g_knorm[l])
        qc_x = rope_2d(qc_x, tabs)
        kc_x = rope_2d(kc_x, tabs)

        oa_x = diff_attend(qa_x, jnp.concatenate([ka_x, ka_y], axis=1), jnp.concatenate([va_x, va_y], axis=1), lam)
        ob_x = gqa_attend(qb_x, jnp.concatenate([kb_x, kb_y], axis=1), jnp.concatenate([vb_x, vb_y], axis=1))
        oc_x = window_attend(qc_x, kc_x, vc_x, kc_y, vc_y, sink[l])
        mix_x = merge_branches(diff_post(oa_x, g_subln[l], lam_init), flat_heads(ob_x), flat_heads(oc_x),
                               gt_x, w_branch[l], w_out[l])
        x = x + gm1 * rms_norm(mix_x, g_post_mix[l])
        x = x + gm2 * rms_norm(sq_relu_mlp(modulate(x, g_pre_ff[l], sh2, sc2), w_ff1[l], w_ff2[l]), g_post_ff[l])

        if l < DEPTH - 1:
            qb_y = rms_norm(qb_y, g_qnorm[l])
            oa_y = diff_attend(qa_y, ka_y, va_y, lam)
            ob_y = gqa_attend(qb_y, kb_y, vb_y)
            oc_y = gqa_attend(qc_y, kc_y, vc_y, sink[l])
            mix_y = merge_branches(diff_post(oa_y, g_subln[l], lam_init), flat_heads(ob_y), flat_heads(oc_y),
                                   gt_y, w_branch[l], w_out[l])
            y = y + cgm1 * rms_norm(mix_y, g_post_mix[l])
            y = y + cgm2 * rms_norm(sq_relu_mlp(modulate(y, g_pre_ff[l], csh2, csc2), w_ff1[l], w_ff2[l]),
                                    g_post_ff[l])
    return x


_drawn_inputs = setup_inputs


def setup_inputs(seed=0):
    import zlib

    import numpy as np

    out = dict(_drawn_inputs(seed))
    spreads = {}
    factors = {'g_pre_mix': 6.953,
     'g_post_mix': 6.845,
     'g_pre_ff': 6.452,
     'g_post_ff': 6.897,
     'g_qnorm': 8.0,
     'g_knorm': 8.0,
     'lam_q1': 5.409,
     'lam_k1': 6.079,
     'lam_q2': 5.041,
     'lam_k2': 5.918,
     'g_subln': 8.0,
     'sink': 8.0}
    for name, (base, spread) in spreads.items():
        noise = np.random.default_rng([zlib.crc32(name.encode()), seed]).standard_normal(out[name].shape)
        drawn = base * np.exp(spread * noise) if base else spread * noise
        out[name] = jnp.asarray(drawn.astype(out[name].dtype))
    for name, factor in factors.items():
        out[name] = (out[name] * factor).astype(out[name].dtype)
    return out
```

```python
import math
from contextlib import ExitStack

import numpy as np

import concourse.bass as bass
from concourse import mybir

F32 = mybir.dt.float32
F32R = mybir.dt.float32r
BF16 = mybir.dt.bfloat16
I32 = mybir.dt.int32
ALU = mybir.AluOpType
ACT = mybir.ActivationFunctionType
AX_X = mybir.AxisListType.X

P = 128
D = 1024
KT = D // P
NX, NY = 256, 256
NTOK = NX + NY
LAYERS = 2
D_FF = 4096
HEAD = 64
GRID_W = 64
ROPE_THETA = 10000.0
EPS = 1e-6
SUBLN_EPS = 1e-5
SCALE = HEAD ** -0.5
MASKED = -1e30

CW = KT * P
SLOTS = 4
ADA_CHUNKS = 6 * KT
ADA_GROUP = 4
PROJ = {0: [("v", 0), ("v", 1), ("v", 2), ("v", 3), ("k", 0), ("k", 1), ("k", 2), ("k", 3),
            ("q", 0), ("q", 1), ("q", 2), ("q", 3)],
        1: [("v", 0), ("k", 0), ("q", 0), ("q", 1), ("q", 2), ("q", 3)],
        2: [("v", 0), ("k", 0), ("q", 0), ("q", 1), ("q", 2), ("q", 3)]}
QUARTERS = D_FF // D
CHUNKS_OF_LAYER = ADA_CHUNKS + sum(map(len, PROJ.values())) + 3 * (KT + KT // 2) + KT + 2 * QUARTERS * KT
NCHUNK = LAYERS * CHUNKS_OF_LAYER
AHEAD = 3

V_BADA = 0
V_GPRE1 = 48
V_GPOST1 = 56
V_GPRE2 = 64
V_GPOST2 = 72
V_GQ = 80
V_GK = 81
V_GSUB = 82
V_SINK = 83
V_LAM = 91
NV = V_LAM + 4 * HEAD
C_COS = 0
C_SIN = C_COS + NX
C_ID = C_SIN + NX
C_MASK = C_ID + P
C_HEADS = C_MASK + 2 * P
C_COMB = C_HEADS + 2
C_ONE = C_COMB + 2
NC = C_ONE + 1


def shape_constants():
    t = np.arange(NX)
    half = HEAD // 2
    inv = np.power(np.float32(ROPE_THETA), -np.arange(0, half, 2, dtype=np.float32) / np.float32(half))
    row = (t // GRID_W).astype(np.float32)
    col = (t % GRID_W).astype(np.float32)
    cos = np.zeros((P, NX), np.float32)
    sin = np.zeros((P, NX), np.float32)
    for p in range(P):
        d = p % HEAD
        pos = row if d < half else col
        ang = (pos * inv[d % (half // 2)]).astype(np.float32)
        cos[p] = np.cos(ang)
        sin[p] = np.sin(ang) * (-1.0 if d % half < half // 2 else 1.0)
    c = np.zeros((P, NC), np.float32)
    c[:, C_COS:C_COS + NX] = cos
    c[:, C_SIN:C_SIN + NX] = sin
    c[:, C_ID:C_ID + P] = np.eye(P)
    q, k = np.arange(P)[:, None], np.arange(P)[None, :]
    c[:, C_MASK:C_MASK + P] = np.where(k > q, MASKED, 0.0)
    c[:, C_MASK + P:C_MASK + 2 * P] = np.where(k < q, MASKED, 0.0)
    c[:HEAD, C_HEADS] = 1.0
    c[HEAD:, C_HEADS + 1] = 1.0
    c[[0, 2], C_COMB] = 1.0
    c[[1, 3], C_COMB + 1] = 1.0
    c[:, C_ONE] = 1.0
    return c


class Place:
    PER_ROUND = {"chunk": 2 * KT, "raw": 16 * 2 * KT // SLOTS, "tile": 2 * KT, "bank": KT, "hidden": KT}

    def __init__(self):
        self.chunk = self.tile = self.turn = self.out = self.map = self.item = self.unit = 0
        self.roped = self.rstd = self.square = self.part = self.x_new = self.sqsum = self.hsq = 0
        self.gate = self.spread = self.hidden = self.split = self.araw = self.scaled = self.merged = self.half = 0
        self.round = None

    def v(self, kind, n):
        return n if self.round is None else self.round * self.PER_ROUND[kind] + n

    def rounds(self, n):
        self.round = None
        self.chunk += (n - 1) * 2 * KT
        self.tile += (n - 1) * 2 * KT
        self.hidden += (n - 1) * KT


def build_trunk(nc, x_in, w_all, vec_in, c_in, const_in, out):
    with ExitStack() as ctx:
        def sb(name, shape, dt=F32):
            return ctx.enter_context(nc.sbuf_tensor(name, shape, dt))

        def sem(name):
            return ctx.enter_context(nc.semaphore(name))

        ps = ctx.enter_context(nc.psum_tensor("ps", [P, 8, 512], F32))
        BANK_S, BANK_T, BANK_O = 2, 6, 7

        raw = sb("raw", [P, SLOTS, CW])
        w_hi = sb("w_hi", [P, SLOTS, CW], F32R)
        w_lo = sb("w_lo", [P, SLOTS, CW], F32R)
        xT = sb("xT", [P, KT, NTOK])
        h_hi = sb("h_hi", [P, KT, NTOK], F32R)
        h_lo = sb("h_lo", [P, KT, NTOK], F32R)
        a_hi = sb("a_hi", [P, KT, NTOK], F32R)
        a_lo = sb("a_lo", [P, KT, NTOK], F32R)
        mix = sb("mix", [P, KT, NTOK])
        q_sb = sb("q_sb", [P, 4, NTOK])
        k_sb = sb("k_sb", [P, 4, NTOK])
        v_sb = sb("v_sb", [P, 4, 4 * P])
        prob = sb("prob", [P, 2, 2, 512])
        probT = sb("probT", [P, 2, 512])
        tmpA = sb("tmpA", [P, 2, 512])
        tmpB = sb("tmpB", [P, 2, 512])
        sqacc = sb("sqacc", [P, 512])
        shuf = sb("shuf", [P, NX])
        ada_row = sb("ada_row", [4, 2, 512])
        const = sb("const", [P, NC])
        idb = sb("idb", [P, P], BF16)
        maskb = sb("maskb", [P, 2, P], BF16)
        vec = sb("vec", [P, LAYERS, NV])
        c_sb = sb("c_sb", [P, KT, 2])
        c_t = sb("c_t", [P, KT, 2])
        c_silu = sb("c_silu", [P, KT, 2])
        c4 = sb("c4", [P, KT, 4], F32R)
        ada = sb("ada", [P, ADA_CHUNKS, 2])
        coef = sb("coef", [P, 4, KT, 2])
        stat = sb("stat", [P, 4, 48])
        lam_t = sb("lam_t", [P, 2, HEAD])
        lam_s = sb("lam_s", [P, 4])
        nlam = sb("nlam", [P, LAYERS])
        gsub = sb("gsub", [P, LAYERS])
        nsink = sb("nsink", [P, LAYERS, 8])
        mx = sb("mx", [P, 2, 2])
        negm = sb("negm", [P, 2, 2])
        sums = sb("sums", [P, 2, 2])
        esink = sb("esink", [P, 2, 2])
        dsink = sb("dsink", [P, 2, 2])
        rsum = sb("rsum", [P, 2, 2])
        ssA = sb("ssA", [P, 16])

        ident = const[:, C_ID:C_ID + P]
        cos = const[:, C_COS:C_COS + NX]
        sin = const[:, C_SIN:C_SIN + NX]
        ones = const[:, C_ONE:C_ONE + 1]
        heads = const[:, C_HEADS:C_HEADS + 2]
        comb = const[0:4, C_COMB:C_COMB + 2]

        small_in = sem("small_in")
        x_in_ready = sem("x_in_ready")
        raw_ready = [sem(f"raw_ready{s}") for s in range(SLOTS)]
        hi_ready = sem("hi_ready")
        lo_ready = sem("lo_ready")
        products = sem("products")
        half_products = sem("half_products")
        tile_free = [sem("tile_free0"), sem("tile_free1")]
        turn_done = sem("turn_done")
        turn_free = sem("turn_free")
        out_done = sem("out_done")
        out_free = sem("out_free")
        merged = sem("merged")
        scores_done = sem("scores_done")
        exp_done = sem("exp_done")
        max_done = sem("max_done")
        bound_ready = sem("bound_ready")
        dsink_ready = sem("dsink_ready")
        esink_ready = sem("esink_ready")
        probs_ready = sem("probs_ready")
        out_hi = sem("out_hi")
        a_squares = sem("a_squares")
        a_scaled = sem("a_scaled")
        roped = sem("roped")
        zeroed = sem("zeroed")
        rstd_ready = sem("rstd_ready")
        head_sq = sem("head_sq")
        head_summed = sem("head_summed")
        spread = sem("spread")
        sq_ready = sem("sq_ready")
        sqacc_added = sem("sqacc_added")
        scaled = sem("scaled")
        part_hi = sem("part_hi")
        part_ready = sem("part_ready")
        x_new = sem("x_new")
        gate_ready = sem("gate_ready")
        relu_ready = sem("relu_ready")
        hidden_hi = sem("hidden_hi")
        hidden_ready = sem("hidden_ready")
        c_tanh = sem("c_tanh")
        c_ready = sem("c_ready")
        c4_hi = sem("c4_hi")
        c4_ready = sem("c4_ready")
        lam_ready = sem("lam_ready")
        lam_exp = sem("lam_exp")
        tables = sem("tables")
        dve_link = sem("dve_link")
        act_link = sem("act_link")
        stored = sem("stored")

        def tokens(l):
            return NTOK if l < LAYERS - 1 else NX

        def halves(n):
            return [(0, 0, NX)] if n == NX else [(0, 0, NX), (1, NX, NTOK)]

        def units(l):
            return [(t, qt) for t in range(4) for qt in range(tokens(l) // P)]

        def keys(qt):
            return (0, NTOK) if qt < NX // P else (NX, NTOK)

        def n_items(b):
            return 1 if b == 0 else 2

        SH1, SC1, GM1, SH2, SC2, GM2 = (j * KT for j in range(6))
        n_out = KT

        block = ctx.enter_context(nc.Block())

        @block.sync
        def _(sp):
            sp.dma_start(c_sb[:], c_in).then_inc(small_in, 16)
            sp.dma_start(const[:], const_in).then_inc(small_in, 16)
            sp.dma_start(vec[:], vec_in).then_inc(small_in, 16)
            for s in range(SLOTS):
                sp.dma_start(raw[:, s], w_all[s]).then_inc(raw_ready[s], 16)
            sp.dma_start(xT[:], x_in).then_inc(x_in_ready, 16)
            with sp.Fori(1, NCHUNK // SLOTS) as r:
                for s in range(SLOTS):
                    sp.wait_ge(lo_ready, r * SLOTS + (s + 1 - SLOTS))
                    sp.dma_start(raw[:, s], w_all[bass.ds(r * SLOTS + s, 1)].rearrange("a p n -> p (a n)")
                                 ).then_inc(raw_ready[s], 16)
            for k in range(KT):
                sp.wait_ge(x_new, KT * (2 * LAYERS - 1) + k + 1)
                sp.dma_start(out[:, k], xT[:, k, 0:NX]).then_inc(stored, 16)
            sp.wait_ge(stored, 16 * KT)

        @block.gpsimd
        def _(pool):
            with pool.Fori(0, NCHUNK // SLOTS) as r:
                for s in range(SLOTS):
                    pool.wait_ge(hi_ready, r * SLOTS + (s + 1))
                    nc.gpsimd.tensor_tensor(w_lo[:, s], raw[:, s], w_hi[:, s].bitcast(F32),
                                            ALU.subtract).then_inc(lo_ready, 1)

        @block.scalar
        def _(act):
            at = Place()
            links = [0]

            def link(ins):
                links[0] += 1
                ins.then_inc(act_link, 1)
                act.wait_ge(act_link, links[0])

            def high_part(c):
                act.wait_ge(raw_ready[c % SLOTS], at.v("raw", 16 * (c // SLOTS + 1)))
                if c >= SLOTS:
                    act.wait_ge(products, at.v("chunk", c - SLOTS + 1))
                nc.scalar.activation(w_hi[:, c % SLOTS], raw[:, c % SLOTS], ACT.Copy).then_inc(hi_ready, 1)

            def next_chunk():
                if at.chunk + AHEAD < NCHUNK:
                    high_part(at.chunk + AHEAD)
                at.chunk += 1

            def silu_c():
                act.wait_ge(small_in, 48)
                nc.scalar.activation(c_t[:], c_sb[:], ACT.Tanh, scale=0.5).then_inc(c_tanh, 1)
                act.wait_ge(c_ready, 1)
                nc.scalar.activation(c4[:, :, 0:2], c_silu[:], ACT.Copy).then_inc(c4_hi, 1)
                act.wait_ge(lam_ready, 1)
                nc.scalar.activation(lam_s[:], lam_s[:], ACT.Exp).then_inc(lam_exp, 1)

            def modulation():
                for _ in range(ADA_CHUNKS // ADA_GROUP):
                    for _ in range(ADA_GROUP):
                        next_chunk()
                    at.tile += 1
                    at.out += 1

            def squares(n, src, ready):
                for k in range(KT):
                    ready(k)
                    if k >= 3:
                        act.wait_ge(sqacc_added, at.sqsum * (KT - 1) + k - 2)
                    dst = sqacc[:, 0:n] if k == 0 else tmpB[:, k % 2, 0:n]
                    nc.scalar.activation(dst, src(k), ACT.Square).then_inc(sq_ready, 1)
                    at.square += 1
                at.sqsum += 1

            def norm_in(n, shift_at):
                at.out += 1
                at.turn += 1
                for k in range(KT):
                    at.scaled += 1
                    act.wait_ge(scaled, at.scaled)
                    for s, a, z in halves(n):
                        ins = nc.scalar.activation(h_hi[:, k, a:z], tmpA[:, k % 2, a:z], ACT.Identity,
                                                   bias=ada[:, shift_at + k, s:s + 1])
                    ins.then_inc(part_hi, 1)
                    at.part += 1

            def turned_values(b, t):
                act.wait_ge(turn_done, at.turn + 1)
                src = ps[:, BANK_T].rearrange("p (k e) -> p k e", e=P)
                if b == 0:
                    ins = nc.scalar.activation(v_sb[:, :, t * P:(t + 1) * P], src, ACT.Copy)
                else:
                    ins = nc.scalar.activation(
                        v_sb[:, :, 0:2 * P].rearrange("p k (h e) -> p k h e", h=2)[:, :, :, 0:HEAD],
                        src.rearrange("p k (h e) -> p k h e", h=2), ACT.Copy)
                ins.then_inc(turn_free, 1)
                at.turn += 1

            def project(l, b):
                n = tokens(l)
                pending = None
                of_b = 0
                for kind, t in PROJ[b]:
                    next_chunk()
                    m = n if kind == "q" else NTOK
                    bank = at.tile % 2
                    dst = {"q": q_sb, "k": k_sb}[kind][:, t, 0:m] if kind != "v" else prob[:, 0, t % 2]
                    act.wait_ge(products, at.chunk)
                    nc.scalar.activation(dst, ps[:, bank, 0:m], ACT.Copy).then_inc(tile_free[bank], 1)
                    if b == 1 and kind != "v":
                        act.wait_ge(tile_free[bank], at.tile // 2 + 1)
                        if of_b >= 2:
                            act.wait_ge(head_summed, l * (len(PROJ[1]) - 2) + of_b - 1)
                        nc.scalar.activation(tmpB[:, of_b % 2, 0:m], dst, ACT.Square).then_inc(head_sq, 1)
                        of_b += 1
                    at.tile += 1
                    if pending is not None:
                        turned_values(b, pending)
                    pending = t if kind == "v" else None
                if b == 1:
                    at.out += 1
                    at.turn += len(PROJ[1]) - 1

            def attend(l, b):
                todo = units(l)
                per = n_items(b)

                def exponentials(i):
                    t, qt = todo[i]
                    a, z = keys(qt)
                    slot = at.unit % 2
                    act.wait_ge(bound_ready, at.unit + 1)
                    for m in range(2):
                        nc.scalar.activation(prob[:, slot, m, a:z], ps[:, BANK_S + at.map % 4, a:z], ACT.Exp,
                                             bias=negm[:, slot, m:m + 1], scale=SCALE,
                                             accum_out=sums[:, slot, m:m + 1]).then_inc(exp_done, 1)
                        at.map += 1
                    if b == 2:
                        act.wait_ge(dsink_ready, at.gate + 1)
                        nc.scalar.activation(esink[:, slot], dsink[:, slot], ACT.Exp).then_inc(esink_ready, 1)
                        at.gate += 1
                    at.unit += 1

                def output(i):
                    t, qt = todo[i]
                    act.wait_ge(out_done, at.out + 1)
                    if b == 0:
                        dst = mix[:, qt, t * P:(t + 1) * P]
                        nc.scalar.activation(dst, ps[:, BANK_O, 0:P], ACT.Copy).then_inc(out_free, 1)
                        act.wait_ge(out_free, at.out + 1)
                        nc.scalar.activation(tmpB[:, 0, 0:P], dst, ACT.Square,
                                             accum_out=ssA[:, i:i + 1]).then_inc(a_squares, 1)
                    else:
                        nc.scalar.activation(a_hi[:, t, qt * P:(qt + 1) * P], ps[:, BANK_O, 0:P],
                                             ACT.Copy).then_inc(out_hi, 1)
                    at.out += 1

                exponentials(0)
                for i, (t, qt) in enumerate(todo):
                    if i + 1 < len(todo):
                        exponentials(i + 1)
                    a, z = keys(qt)
                    for j in range(per):
                        act.wait_ge(turn_done, at.turn + 1)
                        nc.scalar.activation(probT[:, at.turn % 2, a:z], ps[:, BANK_T, a:z],
                                             ACT.Copy).then_inc(turn_free, 1)
                        at.turn += 1
                        if j == 0 and i >= 1:
                            output(i - 1)
                output(len(todo) - 1)
                if b == 0:
                    n = tokens(l)
                    for t in range(4):
                        act.wait_ge(turn_done, at.turn + 1)
                        nc.scalar.activation(a_hi[:, t, 0:n], ps[:, BANK_T, 0:n], ACT.Copy,
                                             scale=gsub[:, l:l + 1]).then_inc(out_hi, 1)
                        at.turn += 1

            def merge(l, b):
                n = tokens(l)
                for pair in range(KT // 2):
                    for j in range(2):
                        next_chunk()
                        act.wait_ge(products, at.chunk)
                        nc.scalar.activation(tmpB[:, j, 0:n], ps[:, at.tile % 2, 0:n], ACT.Tanh,
                                             scale=0.5).then_inc(tile_free[at.tile % 2], 1)
                        at.tile += 1
                    next_chunk()
                    at.tile += 2

            def split_merged(n):
                for k in range(KT):
                    at.merged += 1
                    act.wait_ge(merged, at.merged)
                    nc.scalar.activation(h_hi[:, k, 0:n], mix[:, k, 0:n], ACT.Copy, scale=0.5).then_inc(part_hi, 1)
                    at.part += 1

            def project_out(n):
                for k in range(KT):
                    next_chunk()
                    act.wait_ge(products, at.chunk)
                    if k >= 3:
                        act.wait_ge(sqacc_added, at.sqsum * (KT - 1) + k - 2)
                    dst = sqacc[:, 0:n] if k == 0 else tmpB[:, k % 2, 0:n]
                    nc.scalar.activation(dst, ps[:, at.tile % 2, 0:n], ACT.Square).then_inc(sq_ready, 1)
                    at.tile += 1
                    at.square += 1
                at.sqsum += 1

            def norm_out(n, squares_for):
                at.out += 1
                at.turn += 1
                if squares_for:
                    base = at.x_new
                    squares(squares_for, lambda k: xT[:, k, 0:squares_for],
                            lambda k: act.wait_ge(x_new, base + k + 1))
                at.x_new += KT

            def quarter(n, last):
                for j in range(KT):
                    next_chunk()
                    bank = at.tile % 2
                    act.wait_ge(products, at.v("chunk", at.chunk))
                    nc.scalar.activation(tmpB[:, j % 2, 0:n], ps[:, bank, 0:n], ACT.Relu).then_inc(relu_ready, 1)
                    at.tile += 1
                    at.hidden += 1
                    act.wait_ge(relu_ready, at.v("hidden", at.hidden))
                    nc.scalar.activation(a_hi[:, j, 0:n], tmpB[:, j % 2, 0:n], ACT.Square).then_inc(hidden_hi, 1)
                for k in range(KT):
                    next_chunk()
                    if last:
                        act.wait_ge(tile_free[at.tile % 2], at.tile // 2 + 1)
                        if k >= 3:
                            act.wait_ge(sqacc_added, at.sqsum * (KT - 1) + k - 2)
                        dst = sqacc[:, 0:n] if k == 0 else tmpB[:, k % 2, 0:n]
                        nc.scalar.activation(dst, mix[:, k, 0:n], ACT.Square).then_inc(sq_ready, 1)
                        at.square += 1
                    at.tile += 1
                if last:
                    at.sqsum += 1

            def mlp(n):
                with act.Fori(0, QUARTERS - 1) as at.round:
                    quarter(n, False)
                at.rounds(QUARTERS - 1)
                quarter(n, True)

            for c in range(AHEAD):
                high_part(c)
            silu_c()
            act.wait_ge(x_in_ready, 16)
            squares(NTOK, lambda k: xT[:, k], lambda k: None)
            for l in range(LAYERS):
                n = tokens(l)
                modulation()
                norm_in(NTOK, SH1)
                for b in range(3):
                    project(l, b)
                    attend(l, b)
                    merge(l, b)
                split_merged(n)
                project_out(n)
                norm_out(n, n)
                norm_in(n, SH2)
                mlp(n)
                norm_out(n, NTOK if l < LAYERS - 1 else 0)

        @block.vector
        def _(dve):
            at = Place()
            links = [0]

            def link(ins):
                links[0] += 1
                ins.then_inc(dve_link, 1)
                dve.wait_ge(dve_link, links[0])

            def setup():
                dve.wait_ge(small_in, 48)
                nc.vector.tensor_copy(idb[:], ident)
                nc.vector.tensor_copy(maskb[:].rearrange("p a b -> p (a b)"),
                                      const[:, C_MASK:C_MASK + 2 * P]).then_inc(tables, 1)
                dve.wait_ge(c_tanh, 1)
                link(nc.vector.scalar_tensor_tensor(out=c_silu[:], in0=c_t[:], scalar=1.0, in1=c_sb[:],
                                                    op0=ALU.add, op1=ALU.mult))
                nc.vector.tensor_scalar(c_silu[:], c_silu[:], 0.5, None, ALU.mult).then_inc(c_ready, 1)
                dve.wait_ge(c4_hi, 1)
                nc.vector.tensor_tensor(c4[:, :, 2:4], c_silu[:], c4[:, :, 0:2].bitcast(F32),
                                        ALU.subtract).then_inc(c4_ready, 1)
                for l in range(LAYERS):
                    v = vec[:, l, V_LAM:V_LAM + 4 * HEAD].rearrange("p (a b d) -> p a b d", a=2, b=2)
                    link(nc.vector.tensor_tensor(lam_t[:], v[:, :, 0], v[:, :, 1], ALU.mult))
                    link(nc.vector.reduce_sum(lam_s[:, 2 * l:2 * l + 2], lam_t[:], AX_X))
                nc.vector.tensor_scalar(lam_s[:], lam_s[:], 1.0, None, ALU.mult).then_inc(lam_ready, 1)
                dve.wait_ge(lam_exp, 1)
                for l in range(LAYERS):
                    lam_init = 0.8 - 0.6 * math.exp(-0.3 * l)
                    link(nc.vector.tensor_tensor(nlam[:, l:l + 1], lam_s[:, 2 * l + 1:2 * l + 2],
                                                 lam_s[:, 2 * l:2 * l + 1], ALU.subtract))
                    link(nc.vector.tensor_scalar(nlam[:, l:l + 1], nlam[:, l:l + 1], -lam_init, None, ALU.add))
                    link(nc.vector.tensor_scalar(gsub[:, l:l + 1], vec[:, l, V_GSUB:V_GSUB + 1], 1.0 - lam_init,
                                                 None, ALU.mult))
                    link(nc.vector.tensor_scalar(nsink[:, l], vec[:, l, V_SINK:V_SINK + 8], -1.0, None, ALU.mult))

            def add_squares(n, k):
                dve.wait_ge(sq_ready, at.square + k + 1)
                if k > 1:
                    dve.wait_ge(sqacc_added, at.sqsum * (KT - 1) + k - 1)
                nc.vector.tensor_tensor(sqacc[:, 0:n], sqacc[:, 0:n], tmpB[:, k % 2, 0:n],
                                        ALU.add).then_inc(sqacc_added, 1)
                if k == KT - 1:
                    at.square += KT
                    at.sqsum += 1

            def rstd(src, ncol, inv, eps, frees_out):
                v, nh, y, t = (stat[:, j, 0:ncol] for j in range(4))
                ins = nc.vector.tensor_scalar(v, src, inv, eps, ALU.mult, ALU.add)
                if frees_out:
                    ins.then_inc(out_free, 1)
                    at.out += 1
                    dve.wait_ge(out_free, at.out)
                else:
                    link(ins)
                nc.vector.tensor_scalar(nh, v, -0.5, None, ALU.mult)
                link(nc.vector.tensor_scalar(t.bitcast(I32), v.bitcast(I32), 1, None, ALU.logical_shift_right))
                link(nc.vector.tensor_scalar(y.bitcast(I32), t.bitcast(I32), -1.0, float(0x5F3759DF), ALU.mult,
                                             ALU.add))
                for j in range(3):
                    link(nc.vector.tensor_tensor(t, y, y, ALU.mult))
                    link(nc.vector.tensor_tensor(t, t, nh, ALU.mult))
                    ins = nc.vector.scalar_tensor_tensor(out=y, in0=t, scalar=1.5, in1=y, op0=ALU.add, op1=ALU.mult)
                    if j < 2:
                        link(ins)
                ins.then_inc(rstd_ready, 1)
                at.rstd += 1
                dve.wait_ge(rstd_ready, at.rstd)
                return y

            def modulation(l):
                groups = ADA_CHUNKS // ADA_GROUP

                def rows(g):
                    bank = at.tile % 2
                    at.chunk += ADA_GROUP
                    dve.wait_ge(products, at.chunk)
                    nc.vector.tensor_copy(ada_row[:, g % 2], ps[0:4, bank]).then_inc(tile_free[bank], 1)
                    at.tile += 1

                def columns(g):
                    c = g * ADA_GROUP
                    dve.wait_ge(out_done, at.out + 1)
                    nc.vector.tensor_tensor(
                        ada[:, c:c + ADA_GROUP], ps[:, BANK_O, 0:2 * ADA_GROUP].rearrange("p (c s) -> p c s", s=2),
                        vec[:, l, V_BADA + c:V_BADA + c + ADA_GROUP].unsqueeze(2).to_broadcast([P, ADA_GROUP, 2]),
                        ALU.add).then_inc(out_free, 1)
                    at.out += 1

                for g in range(groups):
                    rows(g)
                    if g:
                        columns(g - 1)
                columns(groups - 1)
                dve.wait_ge(out_free, at.out)

                def gain(col):
                    return vec[:, l, col:col + KT].unsqueeze(2).to_broadcast([P, KT, 2])

                for j, (scale_at, gate_at, pre, post) in enumerate(((SC1, GM1, V_GPRE1, V_GPOST1),
                                                                    (SC2, GM2, V_GPRE2, V_GPOST2))):
                    link(nc.vector.scalar_tensor_tensor(out=coef[:, 2 * j], in0=ada[:, scale_at:scale_at + KT],
                                                        scalar=1.0, in1=gain(pre), op0=ALU.add, op1=ALU.mult))
                    link(nc.vector.tensor_tensor(coef[:, 2 * j + 1], ada[:, gate_at:gate_at + KT], gain(post),
                                                 ALU.mult))

            def token_rstd(n):
                dve.wait_ge(out_done, at.out + 1)
                rstd(ps[:, BANK_O, 0:n // P], n // P, 1.0 / D, EPS, True)
                dve.wait_ge(turn_done, at.turn + 1)

            def norm_in(n, which, shift_at):
                token_rstd(n)

                def scale(k):
                    if k >= 2:
                        dve.wait_ge(part_ready, at.part)
                    for s, a, z in halves(n):
                        ins = nc.vector.scalar_tensor_tensor(
                            out=tmpA[:, k % 2, a:z], in0=xT[:, k, a:z], scalar=coef[:, which, k, s:s + 1],
                            in1=ps[:, BANK_T, a:z], op0=ALU.mult, op1=ALU.mult)
                    ins.then_inc(scaled, 1)

                def low(k):
                    dve.wait_ge(part_hi, at.part + 1)
                    for s, a, z in halves(n):
                        ins = nc.vector.scalar_tensor_tensor(
                            out=h_lo[:, k, a:z], in0=tmpA[:, k % 2, a:z], scalar=ada[:, shift_at + k, s:s + 1],
                            in1=h_hi[:, k, a:z].bitcast(F32), op0=ALU.add, op1=ALU.subtract)
                    ins.then_inc(part_ready, 1)
                    at.part += 1

                for k in range(KT):
                    scale(k)
                    if k:
                        low(k - 1)
                low(KT - 1)
                at.scaled += KT
                dve.wait_ge(scaled, at.scaled)
                dve.sem_inc(turn_free, 1)
                at.turn += 1

            def norm_out(n, which, squares_for):
                token_rstd(n)
                for k in range(KT):
                    for s, a, z in halves(n):
                        ins = nc.vector.scalar_tensor_tensor(
                            out=tmpA[:, k % 2, a:z], in0=mix[:, k, a:z], scalar=coef[:, which, k, s:s + 1],
                            in1=ps[:, BANK_T, a:z], op0=ALU.mult, op1=ALU.mult)
                    if k == KT - 1:
                        ins.then_inc(turn_free, 1)
                        at.turn += 1
                        dve.wait_ge(turn_free, at.turn)
                    else:
                        link(ins)
                    nc.vector.tensor_tensor(xT[:, k, 0:n], xT[:, k, 0:n], tmpA[:, k % 2, 0:n],
                                            ALU.add).then_inc(x_new, 1)
                    if squares_for and k > 1:
                        add_squares(squares_for, k - 1)
                if squares_for:
                    add_squares(squares_for, KT - 1)

            def rope(dst):
                x = dst[:, 0:NX]
                if at.roped:
                    dve.wait_ge(roped, at.roped)
                link(nc.vector.stream_shuffle(shuf[:], x, [(j + 16) % 32 for j in range(32)]))
                nc.vector.tensor_tensor(x, x, cos, ALU.mult)
                link(nc.vector.tensor_tensor(shuf[:], shuf[:], sin, ALU.mult))
                nc.vector.tensor_tensor(x, x, shuf[:], ALU.add).then_inc(roped, 1)
                at.roped += 1

            def project(l, b):
                n = tokens(l)
                if b == 1:
                    nc.vector.memset(v_sb[:, :, HEAD:2 * HEAD], 0.0).then_inc(zeroed, 1)
                at.chunk += len(PROJ[b])
                for kind, t in PROJ[b]:
                    if kind == "v":
                        at.turn += 1
                    elif b != 1:
                        dve.wait_ge(tile_free[at.tile % 2], at.tile // 2 + 1)
                        rope({"q": q_sb, "k": k_sb}[kind][:, t])
                    at.tile += 1
                if b != 1:
                    return
                tiles = [(k_sb, 0, NTOK, V_GK)] + [(q_sb, t, n, V_GQ) for t in range(4)]
                starts = [0]
                for _, _, m, _ in tiles:
                    starts.append(starts[-1] + 2 * m // P)
                dve.wait_ge(out_done, at.out + 1)
                y = rstd(ps[:, BANK_O, 0:starts[-1]], starts[-1], 1.0 / HEAD, EPS, True)

                def expand(j):
                    tt = tiles[j][2] // P
                    src = y[:, starts[j]:starts[j + 1]].rearrange("p (t h) -> p t h", h=2)
                    nc.vector.tensor_copy(tmpA[:, j % 2, 0:tt * P].rearrange("p (t h d) -> p t h d", t=tt, h=2),
                                          src.unsqueeze(3).to_broadcast([P, tt, 2, HEAD])).then_inc(spread, 1)

                expand(0)
                for j, (buf, t, m, col) in enumerate(tiles):
                    if j + 1 < len(tiles):
                        expand(j + 1)
                    dve.wait_ge(turn_done, at.turn + 1)
                    nc.vector.scalar_tensor_tensor(out=buf[:, t, 0:m], in0=buf[:, t, 0:m],
                                                   scalar=vec[:, l, col:col + 1], in1=ps[:, BANK_T, 0:m],
                                                   op0=ALU.mult, op1=ALU.mult).then_inc(turn_free, 1)
                    at.turn += 1
                    dve.wait_ge(turn_free, at.turn)
                    rope(buf[:, t])

            def attend(l, b):
                todo = units(l)
                per = n_items(b)
                n = tokens(l)

                def bounds(i):
                    t, qt = todo[i]
                    a, z = keys(qt)
                    slot = at.unit % 2
                    for m in range(2):
                        dve.wait_ge(scores_done, at.map + 1)
                        nc.vector.reduce_max(mx[:, slot, m:m + 1], ps[:, BANK_S + at.map % 4, a:z],
                                             AX_X).then_inc(max_done, 1)
                        at.map += 1
                    dve.wait_ge(max_done, at.map)
                    if b == 2:
                        nc.vector.scalar_tensor_tensor(
                            out=negm[:, slot], in0=mx[:, slot], scalar=-SCALE, in1=nsink[:, l, 2 * t:2 * t + 2],
                            op0=ALU.mult, op1=ALU.min).then_inc(bound_ready, 1)
                        dve.wait_ge(bound_ready, at.unit + 1)
                        nc.vector.tensor_tensor(dsink[:, slot], negm[:, slot], nsink[:, l, 2 * t:2 * t + 2],
                                                ALU.subtract).then_inc(dsink_ready, 1)
                    else:
                        nc.vector.tensor_scalar(negm[:, slot], mx[:, slot], -SCALE, None,
                                                ALU.mult).then_inc(bound_ready, 1)
                    at.unit += 1

                def normalise(i):
                    t, qt = todo[i]
                    a, z = keys(qt)
                    slot = at.item % 2
                    dve.wait_ge(exp_done, 2 * (at.item + 1))
                    if b == 2:
                        dve.wait_ge(esink_ready, at.gate + 1)
                        at.gate += 1
                        link(nc.vector.tensor_tensor(sums[:, slot], sums[:, slot], esink[:, slot], ALU.add))
                    link(nc.vector.reciprocal(rsum[:, slot], sums[:, slot]))
                    e = [prob[:, slot, m, a:z] for m in range(2)]
                    if b == 0:
                        link(nc.vector.tensor_scalar(rsum[:, slot, 1:2], rsum[:, slot, 1:2], nlam[:, l:l + 1], None,
                                                     ALU.mult))
                        link(nc.vector.tensor_scalar(e[0], e[0], rsum[:, slot, 0:1], None, ALU.mult))
                        nc.vector.scalar_tensor_tensor(out=e[0], in0=e[1], scalar=rsum[:, slot, 1:2], in1=e[0],
                                                       op0=ALU.mult, op1=ALU.add).then_inc(probs_ready, 1)
                    else:
                        for m in range(2):
                            nc.vector.tensor_scalar(e[m], e[m], rsum[:, slot, m:m + 1], None,
                                                    ALU.mult).then_inc(probs_ready, 1)
                    at.item += 1

                def output(i):
                    t, qt = todo[i]
                    at.split += 1
                    dve.wait_ge(out_hi, at.split)
                    cols = slice(qt * P, (qt + 1) * P)
                    nc.vector.tensor_tensor(a_lo[:, t, cols], ps[:, BANK_O, 0:P], a_hi[:, t, cols].bitcast(F32),
                                            ALU.subtract).then_inc(out_free, 1)

                bounds(0)
                for i in range(len(todo)):
                    if i + 1 < len(todo):
                        bounds(i + 1)
                    normalise(i)
                    if b and i >= 1:
                        output(i - 1)
                if b:
                    output(len(todo) - 1)
                at.turn += per * len(todo)
                at.out += len(todo)
                if b == 0:
                    at.araw += len(todo)
                    dve.wait_ge(a_squares, at.araw)
                    y = rstd(ssA[:, 0:len(todo)], len(todo), 1.0 / P, SUBLN_EPS, False)
                    for i, (t, qt) in enumerate(todo):
                        dst = mix[:, qt, t * P:(t + 1) * P]
                        nc.vector.tensor_scalar(dst, dst, y[:, i:i + 1], None, ALU.mult).then_inc(a_scaled, 1)
                    for t in range(4):
                        at.split += 1
                        dve.wait_ge(out_hi, at.split)
                        nc.vector.scalar_tensor_tensor(
                            out=a_lo[:, t, 0:n], in0=ps[:, BANK_T, 0:n], scalar=gsub[:, l:l + 1],
                            in1=a_hi[:, t, 0:n].bitcast(F32), op0=ALU.mult, op1=ALU.subtract).then_inc(turn_free, 1)
                        at.turn += 1

            def merge(l, b):
                n = tokens(l)
                for pair in range(KT // 2):
                    gates = at.tile
                    at.tile += 2
                    at.chunk += 3
                    for j in range(2):
                        k = 2 * pair + j
                        dve.wait_ge(tile_free[(gates + j) % 2], (gates + j) // 2 + 1)
                        if j == 0:
                            at.half += 1
                            dve.wait_ge(half_products, at.half)
                        else:
                            dve.wait_ge(products, at.chunk)
                        dst = mix[:, k, 0:n] if b == 0 else tmpA[:, j, 0:n]
                        bank = at.tile % 2
                        nc.vector.scalar_tensor_tensor(
                            out=dst, in0=tmpB[:, j, 0:n], scalar=1.0, in1=ps[:, bank, 0:n],
                            op0=ALU.add, op1=ALU.mult).then_inc(tile_free[bank], 1)
                        if b:
                            dve.wait_ge(tile_free[bank], at.tile // 2 + 1)
                            ins = nc.vector.tensor_tensor(mix[:, k, 0:n], mix[:, k, 0:n], tmpA[:, j, 0:n], ALU.add)
                            if b == 1:
                                link(ins)
                            else:
                                ins.then_inc(merged, 1)
                        at.tile += 1

            def split_merged(n):
                for k in range(KT):
                    dve.wait_ge(part_hi, at.part + 1)
                    ins = nc.vector.scalar_tensor_tensor(
                        out=h_lo[:, k, 0:n], in0=mix[:, k, 0:n], scalar=0.5, in1=h_hi[:, k, 0:n].bitcast(F32),
                        op0=ALU.mult, op1=ALU.subtract)
                    ins.then_inc(part_ready, 1)
                    at.part += 1

            def project_out(n):
                at.chunk += KT
                for k in range(KT):
                    bank = at.tile % 2
                    dve.wait_ge(sq_ready, at.square + k + 1)
                    nc.vector.tensor_copy(mix[:, k, 0:n], ps[:, bank, 0:n]).then_inc(tile_free[bank], 1)
                    at.tile += 1
                    if 1 <= k < KT - 1:
                        add_squares(n, k)
                add_squares(n, KT - 1)

            def quarter(n, last):
                for j in range(KT):
                    bank = at.tile % 2
                    at.hidden += 1
                    dve.wait_ge(relu_ready, at.v("hidden", at.hidden))
                    nc.vector.scalar_tensor_tensor(out=tmpA[:, j % 2, 0:n], in0=ps[:, bank, 0:n], scalar=0.0,
                                                   in1=tmpB[:, j % 2, 0:n], op0=ALU.max,
                                                   op1=ALU.mult).then_inc(tile_free[bank], 1)
                    dve.wait_ge(tile_free[bank], at.v("bank", at.tile // 2 + 1))
                    dve.wait_ge(hidden_hi, at.v("hidden", at.hidden))
                    nc.vector.tensor_tensor(a_lo[:, j, 0:n], tmpA[:, j % 2, 0:n], a_hi[:, j, 0:n].bitcast(F32),
                                            ALU.subtract).then_inc(hidden_ready, 1)
                    at.tile += 1
                at.chunk += KT
                for k in range(KT):
                    bank = at.tile % 2
                    at.chunk += 1
                    dve.wait_ge(products, at.v("chunk", at.chunk))
                    nc.vector.tensor_tensor(mix[:, k, 0:n], mix[:, k, 0:n], ps[:, bank, 0:n],
                                            ALU.add).then_inc(tile_free[bank], 1)
                    at.tile += 1
                    if last and k > 1:
                        add_squares(n, k - 1)
                if last:
                    add_squares(n, KT - 1)

            def mlp(n):
                link(nc.vector.memset(mix[:, :, 0:n], 0.0))
                with dve.Fori(0, QUARTERS - 1) as at.round:
                    quarter(n, False)
                at.rounds(QUARTERS - 1)
                quarter(n, True)

            setup()
            for k in range(1, KT):
                add_squares(NTOK, k)
            for l in range(LAYERS):
                n = tokens(l)
                modulation(l)
                norm_in(NTOK, 0, SH1)
                for b in range(3):
                    project(l, b)
                    attend(l, b)
                    merge(l, b)
                split_merged(n)
                project_out(n)
                norm_out(n, 1, n)
                norm_in(n, 2, SH2)
                mlp(n)
                norm_out(n, 3, NTOK if l < LAYERS - 1 else 0)

        @block.tensor
        def _(pe):
            at = Place()

            def blocks(bank, jobs, hi, lo, n, ready=None):
                slot = at.chunk % SLOTS
                for i, (blk, k) in enumerate(jobs):
                    if ready:
                        ready(k)
                    cols = slice(blk * P, (blk + 1) * P)
                    for p, (w, a) in enumerate(((w_hi, hi), (w_lo, hi), (w_hi, lo))):
                        ins = nc.tensor.matmul(ps[:, bank, 0:n], w[:, slot, cols], a[:, k, 0:n],
                                               start=(i == 0 and p == 0), stop=(i == len(jobs) - 1 and p == 2))
                return ins

            def chunk_wait():
                pe.wait_ge(lo_ready, at.v("chunk", at.chunk + 1))

            def open_tile():
                bank = at.tile % 2
                if at.tile >= 2:
                    pe.wait_ge(tile_free[bank], at.v("bank", at.tile // 2))
                at.tile += 1
                return bank

            def product(hi, lo, n, ready=None):
                chunk_wait()
                blocks(open_tile(), [(k, k) for k in range(KT)], hi, lo, n, ready).then_inc(products, 1)
                at.chunk += 1

            def open_turn():
                if at.turn:
                    pe.wait_ge(turn_free, at.turn)
                at.turn += 1

            def open_out():
                if at.out:
                    pe.wait_ge(out_free, at.out)
                at.out += 1

            def turn(tiles):
                for src, col in tiles:
                    ins = nc.tensor.transpose(ps[:, BANK_T, col:col + P], src, ident)
                ins.then_inc(turn_done, 1)

            def modulation():
                def columns(g, bank, tile):
                    pe.wait_ge(tile_free[bank], tile // 2 + 1)
                    open_out()
                    for j in range(ADA_GROUP):
                        ins = nc.tensor.matmul(ps[:, BANK_O, 2 * j:2 * j + 2], ada_row[:, g % 2, j * P:(j + 1) * P],
                                               comb, start=True, stop=True)
                    ins.then_inc(out_done, 1)

                before = None
                for g in range(ADA_CHUNKS // ADA_GROUP):
                    tile = at.tile
                    bank = open_tile()
                    for j in range(ADA_GROUP):
                        chunk_wait()
                        slot = at.chunk % SLOTS
                        for k in range(KT):
                            for w in (w_hi, w_lo):
                                ins = nc.tensor.matmul(ps[0:4, bank, j * P:(j + 1) * P], c4[:, k],
                                                       w[:, slot, k * P:(k + 1) * P],
                                                       start=(k == 0 and w is w_hi), stop=(k == KT - 1 and w is w_lo))
                        ins.then_inc(products, 1)
                        at.chunk += 1
                    if before:
                        columns(*before)
                    before = (g, bank, tile)
                columns(*before)

            def token_rstd(n):
                at.sqsum += 1
                pe.wait_ge(sqacc_added, at.sqsum * (KT - 1))
                open_out()
                for t in range(n // P):
                    ins = nc.tensor.matmul(ps[:, BANK_O, t:t + 1], sqacc[:, t * P:(t + 1) * P], ones,
                                           start=True, stop=True)
                ins.then_inc(out_done, 1)
                at.rstd += 1
                pe.wait_ge(rstd_ready, at.rstd)
                open_turn()
                turn([(stat[:, 2, t:t + 1].to_broadcast([P, P]), t * P) for t in range(n // P)])

            def next_part(k):
                at.part += 1
                pe.wait_ge(part_ready, at.part)

            def project(l, b):
                n = tokens(l)
                pending = None
                heads_at = of_b = 0

                def turn_values(t, bank, tile):
                    pe.wait_ge(tile_free[bank], tile // 2 + 1)
                    open_turn()
                    turn([(prob[:, 0, t % 2, j * P:(j + 1) * P], j * P) for j in range(NTOK // P)])

                def head_sums(m):
                    nonlocal heads_at, of_b
                    if heads_at == 0:
                        open_out()
                    at.hsq += 1
                    pe.wait_ge(head_sq, at.hsq)
                    for j in range(m // P):
                        ins = nc.tensor.matmul(ps[:, BANK_O, heads_at:heads_at + 2],
                                               tmpB[:, of_b % 2, j * P:(j + 1) * P], heads,
                                               start=True, stop=True)
                        heads_at += 2
                    of_b += 1
                    ins.then_inc(out_done if of_b == len(PROJ[1]) - 1 else head_summed, 1)

                for i, (kind, t) in enumerate(PROJ[b]):
                    tile = at.tile
                    product(h_hi, h_lo, n if kind == "q" else NTOK, next_part if b == 0 and i == 0 else None)
                    if pending:
                        pending()
                    pending = None
                    if kind == "v":
                        pending = lambda t=t, tile=tile: turn_values(t, tile % 2, tile)
                    elif b == 1:
                        pending = lambda m=n if kind == "q" else NTOK: head_sums(m)
                if pending:
                    pending()
                if b == 1:
                    at.rstd += 1
                    pe.wait_ge(rstd_ready, at.rstd)
                    for j, m in enumerate([NTOK] + 4 * [n]):
                        at.spread += 1
                        pe.wait_ge(spread, at.spread)
                        open_turn()
                        turn([(tmpA[:, j % 2, i * P:(i + 1) * P], i * P) for i in range(m // P)])

            def attend(l, b):
                todo = units(l)
                per = n_items(b)
                roped_before = at.roped
                first_q = sum(kind == "k" for kind, _ in PROJ[b])
                at.roped += first_q + 4

                def scores(i):
                    t, qt = todo[i]
                    a, z = keys(qt)
                    kt = t if b == 0 else 0
                    pe.wait_ge(roped, roped_before + first_q + t + 1)
                    window = b == 2 and qt < NX // P
                    for m in range(2):
                        rows = slice(m * HEAD, (m + 1) * HEAD)
                        if at.map >= 4:
                            pe.wait_ge(exp_done, at.map - 3)
                        bank = BANK_S + at.map % 4
                        ins = nc.tensor.matmul(ps[:, bank, a:z], q_sb[rows, t, qt * P:(qt + 1) * P],
                                               k_sb[rows, kt, a:z], start=True, stop=not window)
                        if window:
                            other = (1 - qt) * P
                            ins = nc.tensor.matmul(ps[:, bank, other:other + P], idb[:], maskb[:, qt],
                                                   start=False, stop=True)
                        ins.then_inc(scores_done, 1)
                        at.map += 1

                def turn_probs(i, m):
                    t, qt = todo[i]
                    a, z = keys(qt)
                    at.item += 1
                    pe.wait_ge(probs_ready, at.item)
                    open_turn()
                    turn([(prob[:, (at.unit + i) % 2, m, c:c + P], c) for c in range(a, z, P)])
                    return at.turn - 1

                def weigh(i, m, event):
                    t, qt = todo[i]
                    a, z = keys(qt)
                    pe.wait_ge(turn_free, event + 1)
                    if m == 0:
                        open_out()
                    for c in range(a, z, P):
                        pT = probT[:, event % 2, c:c + P]
                        if b == 0:
                            v = v_sb[:, c // P, t * P:(t + 1) * P]
                            lhs, rhs = pT, v
                        else:
                            lhs, rhs = v_sb[:, c // P, m * HEAD:m * HEAD + P], pT
                        ins = nc.tensor.matmul(ps[:, BANK_O, 0:P], lhs, rhs, start=(c == a and m == 0),
                                               stop=(c == z - P and m == per - 1))
                    if m == per - 1:
                        ins.then_inc(out_done, 1)

                if b == 1:
                    pe.wait_ge(zeroed, l + 1)
                if b == 2 and l == 0:
                    pe.wait_ge(tables, 1)
                scores(0)
                before = None
                for i in range(len(todo)):
                    if i + 1 < len(todo):
                        scores(i + 1)
                    for m in range(per):
                        event = turn_probs(i, m)
                        if before:
                            weigh(*before)
                        before = (i, m, event)
                weigh(*before)
                at.unit += len(todo)
                if b == 0:
                    at.rstd += 1
                    ntt = tokens(l) // P
                    for t in range(4):
                        at.scaled += ntt
                        pe.wait_ge(a_scaled, at.scaled)
                        open_turn()
                        turn([(mix[:, j, t * P:(t + 1) * P], j * P) for j in range(ntt)])

            def merge(l, b):
                n = tokens(l)
                for pair in range(KT // 2):
                    product(h_hi, h_lo, n)
                    product(h_hi, h_lo, n)
                    if pair == 0:
                        pe.wait_ge(turn_free, at.turn)
                        pe.wait_ge(out_free, at.out)
                    chunk_wait()
                    for j in range(2):
                        blocks(open_tile(), [(4 * j + i, i) for i in range(4)], a_hi, a_lo, n
                               ).then_inc(products if j else half_products, 1)
                    at.chunk += 1

            def project_out(n):
                for k in range(KT):
                    product(h_hi, h_lo, n, next_part if k == 0 else None)

            def quarter(n, first):
                for j in range(KT):
                    product(h_hi, h_lo, n, next_part if first and j == 0 else None)

                def next_hidden(k):
                    at.hidden += 1
                    pe.wait_ge(hidden_ready, at.v("hidden", at.hidden))

                for k in range(KT):
                    product(a_hi, a_lo, n, next_hidden if k == 0 else None)

            def mlp(n):
                for k in range(KT):
                    next_part(k)
                with pe.Fori(0, QUARTERS - 1) as at.round:
                    quarter(n, False)
                at.rounds(QUARTERS - 1)
                quarter(n, False)

            pe.wait_ge(small_in, 48)
            pe.wait_ge(c4_ready, 1)
            for l in range(LAYERS):
                n = tokens(l)
                modulation()
                token_rstd(NTOK)
                for b in range(3):
                    project(l, b)
                    attend(l, b)
                    merge(l, b)
                project_out(n)
                token_rstd(n)
                token_rstd(n)
                mlp(n)
                token_rstd(n)


def arrange(inputs):
    def blocks(w):
        return w.reshape(-1, P, P).transpose(1, 0, 2).reshape(P, -1)

    def pair_heads(a, axis):
        a = np.moveaxis(a, axis, 0)
        a = a.reshape((2, 4, HEAD) + a.shape[1:]).swapaxes(0, 1).reshape(a.shape)
        return np.moveaxis(a, 0, axis)

    chunks, vecs = [], []
    for l in range(LAYERS):
        w_ada, w_in, w_branch = inputs["w_ada"][l], inputs["w_in"][l], inputs["w_branch"][l]
        w_out, w1, w2 = inputs["w_out"][l], inputs["w_ff1"][l], inputs["w_ff2"][l]
        cols = lambda w, j: w[:, j * P:(j + 1) * P]
        chunks += [blocks(cols(w_ada, j)) for j in range(ADA_CHUNKS)]
        widths = dict(qa=512, ka=512, va=512, qb=512, kb=P, vb=P, qc=512, kc=P, vc=P, gt=3 * D)
        part, start = {}, 0
        for name, width in widths.items():
            part[name] = w_in[:, start:start + width]
            start += width
        for b, name in enumerate("abc"):
            if b:
                part["q" + name] = pair_heads(part["q" + name], 1)
            wb = w_branch[b * 512:(b + 1) * 512]
            if b:
                wb = pair_heads(wb, 0)
            chunks += [blocks(cols(part[kind + name], t)) for kind, t in PROJ[b]]
            for pair in range(KT // 2):
                chunks += [blocks(cols(part["gt"], b * KT + 2 * pair + j)) for j in range(2)]
                chunks.append(np.concatenate([blocks(cols(wb, 2 * pair + j)) for j in range(2)], 1))
        chunks += [blocks(cols(w_out, j)) for j in range(KT)]
        for r in range(QUARTERS):
            chunks += [blocks(cols(w1, r * KT + j)) for j in range(KT)]
            chunks += [blocks(cols(w2[r * D:(r + 1) * D], j)) for j in range(KT)]
        v = np.zeros((P, NV), np.float32)
        v[:, V_BADA:V_BADA + ADA_CHUNKS] = inputs["b_ada"][l].reshape(-1, P).T
        for col, name in ((V_GPRE1, "g_pre_mix"), (V_GPOST1, "g_post_mix"), (V_GPRE2, "g_pre_ff"),
                          (V_GPOST2, "g_post_ff")):
            v[:, col:col + KT] = inputs[name][l].reshape(KT, P).T
        v[:, V_GQ] = np.tile(inputs["g_qnorm"][l], 2)
        v[:, V_GK] = np.tile(inputs["g_knorm"][l], 2)
        v[:, V_GSUB] = inputs["g_subln"][l]
        v[:, V_SINK:V_SINK + 8] = inputs["sink"][l].reshape(2, 4).T.reshape(1, 8)
        for j, name in enumerate(("lam_q1", "lam_k1", "lam_q2", "lam_k2")):
            v[:, V_LAM + j * HEAD:V_LAM + (j + 1) * HEAD] = inputs[name][l][None]
        vecs.append(v)
    feature_major = lambda a: a.reshape(-1, KT, P).transpose(2, 1, 0)
    x = np.concatenate([inputs["x"][0], inputs["ctx"][0]], 0)
    c = np.concatenate([inputs["c"], inputs["c_ctx"][None]], 0)
    return {
        "x_in": np.ascontiguousarray(feature_major(x)),
        "w_all": np.stack(chunks),
        "vec_in": np.ascontiguousarray(np.stack(vecs, 1)),
        "c_in": np.ascontiguousarray(feature_major(c)),
        "const_in": shape_constants(),
    }


def kernel(**inputs):
    import concourse.bacc as bacc
    from concourse.bass_utils import run_bass_kernel_spmd

    arrays = arrange({k: np.asarray(v) for k, v in inputs.items()})
    nc = bacc.Bacc("TRN2", target_bir_lowering=False, num_devices=1)
    args = [nc.dram_tensor(name, a.shape, F32, kind="ExternalInput").ap() for name, a in arrays.items()]
    args.append(nc.dram_tensor("out", (P, KT, NX), F32, kind="ExternalOutput").ap())
    build_trunk(nc, *args)
    r = run_bass_kernel_spmd(nc, [arrays], core_ids=[0])
    return r.results[0]["out"].transpose(2, 1, 0).reshape(1, NX, D)
```

```python
import math
from contextlib import ExitStack

import numpy as np

import concourse.bass as bass
from concourse import mybir

F32 = mybir.dt.float32
F32R = mybir.dt.float32r
BF16 = mybir.dt.bfloat16
I32 = mybir.dt.int32
ALU = mybir.AluOpType
ACT = mybir.ActivationFunctionType
AX_X = mybir.AxisListType.X

P = 128
D = 1024
KT = D // P
NX, NY = 256, 256
NTOK = NX + NY
LAYERS = 2
D_FF = 4096
HEAD = 64
GRID_W = 64
ROPE_THETA = 10000.0
EPS = 1e-6
SUBLN_EPS = 1e-5
SCALE = HEAD ** -0.5
MASKED = -1e30

CW = KT * P
SLOTS = 4
ADA_CHUNKS = 6 * KT
ADA_GROUP = 4
PROJ = {0: [("v", 0), ("v", 1), ("v", 2), ("v", 3), ("k", 0), ("k", 1), ("k", 2), ("k", 3),
            ("q", 0), ("q", 1), ("q", 2), ("q", 3)],
        1: [("v", 0), ("k", 0), ("q", 0), ("q", 1), ("q", 2), ("q", 3)],
        2: [("v", 0), ("k", 0), ("q", 0), ("q", 1), ("q", 2), ("q", 3)]}
FIRST_GROUPS = 4
FILL = {(0, 0): (0, 4, 8, 1), (0, 1): (0, 8, 12, 1), (0, 2): (1, 0, 4, 1),
        (1, 0): (1, 4, 6, 1), (1, 1): (1, 6, 8, 1), (1, 2): (1, 8, 12, 2)}
QUARTERS = D_FF // D
CHUNKS_OF_LAYER = ADA_CHUNKS + sum(map(len, PROJ.values())) + 3 * (KT + KT // 2) + KT + 2 * QUARTERS * KT
NCHUNK = LAYERS * CHUNKS_OF_LAYER
AHEAD = 3

V_BADA = 0
V_GPRE1 = 48
V_GPOST1 = 56
V_GPRE2 = 64
V_GPOST2 = 72
V_GQ = 80
V_GK = 81
V_GSUB = 82
V_SINK = 83
V_LAM = 91
NV = V_LAM + 4 * HEAD
C_COS = 0
C_SIN = C_COS + NX
C_ID = C_SIN + NX
C_MASK = C_ID + P
C_HEADS = C_MASK + 2 * P
C_COMB = C_HEADS + 2
C_ONE = C_COMB + 2
NC = C_ONE + 1


def shape_constants():
    t = np.arange(NX)
    half = HEAD // 2
    inv = np.power(np.float32(ROPE_THETA), -np.arange(0, half, 2, dtype=np.float32) / np.float32(half))
    row = (t // GRID_W).astype(np.float32)
    col = (t % GRID_W).astype(np.float32)
    cos = np.zeros((P, NX), np.float32)
    sin = np.zeros((P, NX), np.float32)
    for p in range(P):
        d = p % HEAD
        pos = row if d < half else col
        ang = (pos * inv[d % (half // 2)]).astype(np.float32)
        cos[p] = np.cos(ang)
        sin[p] = np.sin(ang) * (-1.0 if d % half < half // 2 else 1.0)
    c = np.zeros((P, NC), np.float32)
    c[:, C_COS:C_COS + NX] = cos
    c[:, C_SIN:C_SIN + NX] = sin
    c[:, C_ID:C_ID + P] = np.eye(P)
    q, k = np.arange(P)[:, None], np.arange(P)[None, :]
    c[:, C_MASK:C_MASK + P] = np.where(k > q, MASKED, 0.0)
    c[:, C_MASK + P:C_MASK + 2 * P] = np.where(k < q, MASKED, 0.0)
    c[:HEAD, C_HEADS] = 1.0
    c[HEAD:, C_HEADS + 1] = 1.0
    c[[0, 2], C_COMB] = 1.0
    c[[1, 3], C_COMB + 1] = 1.0
    c[:, C_ONE] = 1.0
    return c


class Place:
    PER_ROUND = {"chunk": 2 * KT, "raw": 16 * 2 * KT // SLOTS, "tile": 2 * KT, "bank": KT, "hidden": KT}

    def __init__(self):
        self.chunk = self.tile = self.turn = self.out = self.map = self.item = self.unit = 0
        self.roped = self.rstd = self.square = self.part = self.x_new = self.sqsum = self.hsq = 0
        self.gate = self.spread = self.hidden = self.split = self.araw = self.scaled = self.merged = self.half = 0
        self.columns = 0
        self.round = None

    def v(self, kind, n):
        return n if self.round is None else self.round * self.PER_ROUND[kind] + n

    def rounds(self, n):
        self.round = None
        self.chunk += (n - 1) * 2 * KT
        self.tile += (n - 1) * 2 * KT
        self.hidden += (n - 1) * KT


def build_trunk(nc, x_in, w_all, vec_in, c_in, const_in, out):
    with ExitStack() as ctx:
        def sb(name, shape, dt=F32):
            return ctx.enter_context(nc.sbuf_tensor(name, shape, dt))

        def sem(name):
            return ctx.enter_context(nc.semaphore(name))

        ps = ctx.enter_context(nc.psum_tensor("ps", [P, 8, 512], F32))
        BANK_S, BANK_T, BANK_O = 2, 6, 7

        raw = sb("raw", [P, SLOTS, CW])
        w_hi = sb("w_hi", [P, SLOTS, CW], F32R)
        w_lo = sb("w_lo", [P, SLOTS, CW], F32R)
        xT = sb("xT", [P, KT, NTOK])
        h_hi = sb("h_hi", [P, KT, NTOK], F32R)
        h_lo = sb("h_lo", [P, KT, NTOK], F32R)
        a_hi = sb("a_hi", [P, KT, NTOK], F32R)
        a_lo = sb("a_lo", [P, KT, NTOK], F32R)
        mix = sb("mix", [P, KT, NTOK])
        q_sb = sb("q_sb", [P, 4, NTOK])
        k_sb = sb("k_sb", [P, 4, NTOK])
        v_sb = sb("v_sb", [P, 4, 4 * P])
        prob = sb("prob", [P, 2, 2, 512])
        probT = sb("probT", [P, 2, 512])
        tmpA = sb("tmpA", [P, 2, 512])
        tmpB = sb("tmpB", [P, 2, 512])
        sqacc = sb("sqacc", [P, 512])
        shuf = sb("shuf", [P, NX])
        ada_row = sb("ada_row", [4, 2, 512])
        const = sb("const", [P, NC])
        idb = sb("idb", [P, P], BF16)
        maskb = sb("maskb", [P, 2, P], BF16)
        vec = sb("vec", [P, LAYERS, NV])
        c_sb = sb("c_sb", [P, KT, 2])
        c_t = sb("c_t", [P, KT, 2])
        c_silu = sb("c_silu", [P, KT, 2])
        c4 = sb("c4", [P, KT, 4], F32R)
        ada = sb("ada", [P, LAYERS, ADA_CHUNKS, 2])
        coef = sb("coef", [P, LAYERS, 4, KT, 2])
        stat = sb("stat", [P, 4, 48])
        lam_t = sb("lam_t", [P, 2, HEAD])
        lam_s = sb("lam_s", [P, 4])
        nlam = sb("nlam", [P, LAYERS])
        gsub = sb("gsub", [P, LAYERS])
        nsink = sb("nsink", [P, LAYERS, 8])
        mx = sb("mx", [P, 2, 2])
        negm = sb("negm", [P, 2, 2])
        sums = sb("sums", [P, 2, 2])
        esink = sb("esink", [P, 2, 2])
        dsink = sb("dsink", [P, 2, 2])
        rsum = sb("rsum", [P, 2, 2])
        ssA = sb("ssA", [P, 16])

        ident = const[:, C_ID:C_ID + P]
        cos = const[:, C_COS:C_COS + NX]
        sin = const[:, C_SIN:C_SIN + NX]
        ones = const[:, C_ONE:C_ONE + 1]
        heads = const[:, C_HEADS:C_HEADS + 2]
        comb = const[0:4, C_COMB:C_COMB + 2]

        small_in = sem("small_in")
        x_in_ready = sem("x_in_ready")
        raw_ready = [sem(f"raw_ready{s}") for s in range(SLOTS)]
        hi_ready = sem("hi_ready")
        lo_ready = sem("lo_ready")
        products = sem("products")
        half_products = sem("half_products")
        tile_free = [sem("tile_free0"), sem("tile_free1")]
        turn_done = sem("turn_done")
        turn_free = sem("turn_free")
        out_done = sem("out_done")
        out_free = sem("out_free")
        merged = sem("merged")
        columns_done = sem("columns_done")
        scores_done = sem("scores_done")
        exp_done = sem("exp_done")
        max_done = sem("max_done")
        bound_ready = sem("bound_ready")
        dsink_ready = sem("dsink_ready")
        esink_ready = sem("esink_ready")
        probs_ready = sem("probs_ready")
        out_hi = sem("out_hi")
        a_squares = sem("a_squares")
        a_scaled = sem("a_scaled")
        roped = sem("roped")
        zeroed = sem("zeroed")
        rstd_ready = sem("rstd_ready")
        head_sq = sem("head_sq")
        head_summed = sem("head_summed")
        spread = sem("spread")
        sq_ready = sem("sq_ready")
        sqacc_added = sem("sqacc_added")
        scaled = sem("scaled")
        part_hi = sem("part_hi")
        part_ready = sem("part_ready")
        x_new = sem("x_new")
        gate_ready = sem("gate_ready")
        relu_ready = sem("relu_ready")
        hidden_hi = sem("hidden_hi")
        hidden_ready = sem("hidden_ready")
        c_tanh = sem("c_tanh")
        c_ready = sem("c_ready")
        c4_hi = sem("c4_hi")
        c4_ready = sem("c4_ready")
        lam_ready = sem("lam_ready")
        lam_exp = sem("lam_exp")
        tables = sem("tables")
        dve_link = sem("dve_link")
        act_link = sem("act_link")
        stored = sem("stored")

        def tokens(l):
            return NTOK if l < LAYERS - 1 else NX

        def halves(n):
            return [(0, 0, NX)] if n == NX else [(0, 0, NX), (1, NX, NTOK)]

        def units(l):
            return [(t, qt) for t in range(4) for qt in range(tokens(l) // P)]

        def keys(qt):
            return (0, NTOK) if qt < NX // P else (NX, NTOK)

        def n_items(b):
            return 1 if b == 0 else 2

        SH1, SC1, GM1, SH2, SC2, GM2 = (j * KT for j in range(6))
        n_out = KT

        block = ctx.enter_context(nc.Block())

        @block.sync
        def _(sp):
            sp.dma_start(c_sb[:], c_in).then_inc(small_in, 16)
            sp.dma_start(const[:], const_in).then_inc(small_in, 16)
            sp.dma_start(vec[:], vec_in).then_inc(small_in, 16)
            for s in range(SLOTS):
                sp.dma_start(raw[:, s], w_all[s]).then_inc(raw_ready[s], 16)
            sp.dma_start(xT[:], x_in).then_inc(x_in_ready, 16)
            with sp.Fori(1, NCHUNK // SLOTS) as r:
                for s in range(SLOTS):
                    sp.wait_ge(lo_ready, r * SLOTS + (s + 1 - SLOTS))
                    sp.dma_start(raw[:, s], w_all[bass.ds(r * SLOTS + s, 1)].rearrange("a p n -> p (a n)")
                                 ).then_inc(raw_ready[s], 16)
            for k in range(KT):
                sp.wait_ge(x_new, KT * (2 * LAYERS - 1) + k + 1)
                sp.dma_start(out[:, k], xT[:, k, 0:NX]).then_inc(stored, 16)
            sp.wait_ge(stored, 16 * KT)

        @block.gpsimd
        def _(pool):
            with pool.Fori(0, NCHUNK // SLOTS) as r:
                for s in range(SLOTS):
                    pool.wait_ge(hi_ready, r * SLOTS + (s + 1))
                    nc.gpsimd.tensor_tensor(w_lo[:, s], raw[:, s], w_hi[:, s].bitcast(F32),
                                            ALU.subtract).then_inc(lo_ready, 1)

        @block.scalar
        def _(act):
            at = Place()
            links = [0]

            def link(ins):
                links[0] += 1
                ins.then_inc(act_link, 1)
                act.wait_ge(act_link, links[0])

            def high_part(c):
                act.wait_ge(raw_ready[c % SLOTS], at.v("raw", 16 * (c // SLOTS + 1)))
                if c >= SLOTS:
                    act.wait_ge(products, at.v("chunk", c - SLOTS + 1))
                nc.scalar.activation(w_hi[:, c % SLOTS], raw[:, c % SLOTS], ACT.Copy).then_inc(hi_ready, 1)

            def next_chunk():
                if at.chunk + AHEAD < NCHUNK:
                    high_part(at.chunk + AHEAD)
                at.chunk += 1

            def silu_c():
                act.wait_ge(small_in, 48)
                nc.scalar.activation(c_t[:], c_sb[:], ACT.Tanh, scale=0.5).then_inc(c_tanh, 1)
                act.wait_ge(c_ready, 1)
                nc.scalar.activation(c4[:, :, 0:2], c_silu[:], ACT.Copy).then_inc(c4_hi, 1)
                act.wait_ge(lam_ready, 1)
                nc.scalar.activation(lam_s[:], lam_s[:], ACT.Exp).then_inc(lam_exp, 1)

            def modulation(groups):
                for _ in range(groups):
                    for _ in range(ADA_GROUP):
                        next_chunk()
                    at.tile += 2

            def squares(n, src, ready):
                for k in range(KT):
                    ready(k)
                    if k >= 3:
                        act.wait_ge(sqacc_added, at.sqsum * (KT - 1) + k - 2)
                    dst = sqacc[:, 0:n] if k == 0 else tmpB[:, k % 2, 0:n]
                    nc.scalar.activation(dst, src(k), ACT.Square).then_inc(sq_ready, 1)
                    at.square += 1
                at.sqsum += 1

            def norm_in(l, n, shift_at):
                at.out += 1
                at.turn += 1
                for k in range(KT):
                    at.scaled += 1
                    act.wait_ge(scaled, at.scaled)
                    for s, a, z in halves(n):
                        ins = nc.scalar.activation(h_hi[:, k, a:z], tmpA[:, k % 2, a:z], ACT.Identity,
                                                   bias=ada[:, l, shift_at + k, s:s + 1])
                    ins.then_inc(part_hi, 1)
                    at.part += 1

            def turned_values(b, t):
                act.wait_ge(turn_done, at.turn + 1)
                src = ps[:, BANK_T].rearrange("p (k e) -> p k e", e=P)
                if b == 0:
                    ins = nc.scalar.activation(v_sb[:, :, t * P:(t + 1) * P], src, ACT.Copy)
                else:
                    ins = nc.scalar.activation(
                        v_sb[:, :, 0:2 * P].rearrange("p k (h e) -> p k h e", h=2)[:, :, :, 0:HEAD],
                        src.rearrange("p k (h e) -> p k h e", h=2), ACT.Copy)
                ins.then_inc(turn_free, 1)
                at.turn += 1

            def project(l, b):
                n = tokens(l)
                pending = None
                of_b = 0
                for kind, t in PROJ[b]:
                    next_chunk()
                    m = n if kind == "q" else NTOK
                    bank = at.tile % 2
                    dst = {"q": q_sb, "k": k_sb}[kind][:, t, 0:m] if kind != "v" else prob[:, 0, t % 2]
                    act.wait_ge(products, at.chunk)
                    nc.scalar.activation(dst, ps[:, bank, 0:m], ACT.Copy).then_inc(tile_free[bank], 1)
                    if b == 1 and kind != "v":
                        act.wait_ge(tile_free[bank], at.tile // 2 + 1)
                        if of_b >= 2:
                            act.wait_ge(head_summed, l * (len(PROJ[1]) - 2) + of_b - 1)
                        nc.scalar.activation(tmpB[:, of_b % 2, 0:m], dst, ACT.Square).then_inc(head_sq, 1)
                        of_b += 1
                    at.tile += 1
                    if pending is not None:
                        turned_values(b, pending)
                    pending = t if kind == "v" else None
                if b == 1:
                    at.out += 1
                    at.turn += 2

            def attend(l, b):
                todo = units(l)
                per = n_items(b)

                def exponentials(i):
                    t, qt = todo[i]
                    a, z = keys(qt)
                    slot = at.unit % 2
                    act.wait_ge(bound_ready, at.unit + 1)
                    for m in range(2):
                        nc.scalar.activation(prob[:, slot, m, a:z], ps[:, BANK_S + at.map % 4, a:z], ACT.Exp,
                                             bias=negm[:, slot, m:m + 1], scale=SCALE,
                                             accum_out=sums[:, slot, m:m + 1]).then_inc(exp_done, 1)
                        at.map += 1
                    if b == 2:
                        act.wait_ge(dsink_ready, at.gate + 1)
                        nc.scalar.activation(esink[:, slot], dsink[:, slot], ACT.Exp).then_inc(esink_ready, 1)
                        at.gate += 1
                    at.unit += 1

                def output(i):
                    t, qt = todo[i]
                    act.wait_ge(out_done, at.out + 1)
                    if b == 0:
                        dst = mix[:, qt, t * P:(t + 1) * P]
                        nc.scalar.activation(dst, ps[:, BANK_O, 0:P], ACT.Copy).then_inc(out_free, 1)
                        act.wait_ge(out_free, at.out + 1)
                        nc.scalar.activation(tmpB[:, 0, 0:P], dst, ACT.Square,
                                             accum_out=ssA[:, i:i + 1]).then_inc(a_squares, 1)
                    else:
                        nc.scalar.activation(a_hi[:, t, qt * P:(qt + 1) * P], ps[:, BANK_O, 0:P],
                                             ACT.Copy).then_inc(out_hi, 1)
                    at.out += 1

                _, first, end, chunks = FILL[l, b]
                exponentials(0)
                for i, (t, qt) in enumerate(todo):
                    a, z = keys(qt)
                    for j in range(per):
                        act.wait_ge(turn_done, at.turn + 1)
                        nc.scalar.activation(probT[:, at.item % 2, a:z], ps[:, BANK_T, a:z],
                                             ACT.Copy).then_inc(turn_free, 1)
                        at.turn += 1
                        at.item += 1
                        if j == 0 and i >= 1:
                            output(i - 1)
                    if i + 1 < len(todo):
                        exponentials(i + 1)
                    for _ in range(chunks):
                        next_chunk()
                    if b == 1 and qt == 0 and t < 3:
                        at.turn += 1
                output(len(todo) - 1)
                if b == 0:
                    at.araw += len(todo)
                    act.wait_ge(a_squares, at.araw)
                at.tile += 2 * (end - first)

            def turned_a(l):
                n = tokens(l)
                for t in range(4):
                    act.wait_ge(turn_done, at.turn + 1)
                    nc.scalar.activation(a_hi[:, t, 0:n], ps[:, BANK_T, 0:n], ACT.Copy,
                                         scale=gsub[:, l:l + 1]).then_inc(out_hi, 1)
                    at.turn += 1

            def merge(l, b):
                n = tokens(l)
                for pair in range(KT // 2):
                    for j in range(2):
                        next_chunk()
                        act.wait_ge(products, at.chunk)
                        nc.scalar.activation(tmpB[:, j, 0:n], ps[:, at.tile % 2, 0:n], ACT.Tanh,
                                             scale=0.5).then_inc(tile_free[at.tile % 2], 1)
                        at.tile += 1
                    if b == 0 and pair == 0:
                        turned_a(l)
                    next_chunk()
                    at.tile += 2

            def split_merged(n):
                for k in range(KT):
                    at.merged += 1
                    act.wait_ge(merged, at.merged)
                    nc.scalar.activation(h_hi[:, k, 0:n], mix[:, k, 0:n], ACT.Copy, scale=0.5).then_inc(part_hi, 1)
                    at.part += 1

            def project_out(n):
                for k in range(KT):
                    next_chunk()
                    act.wait_ge(products, at.chunk)
                    if k >= 3:
                        act.wait_ge(sqacc_added, at.sqsum * (KT - 1) + k - 2)
                    dst = sqacc[:, 0:n] if k == 0 else tmpB[:, k % 2, 0:n]
                    nc.scalar.activation(dst, ps[:, at.tile % 2, 0:n], ACT.Square).then_inc(sq_ready, 1)
                    at.tile += 1
                    at.square += 1
                at.sqsum += 1

            def norm_out(n, squares_for):
                at.out += 1
                at.turn += 1
                if squares_for:
                    base = at.x_new
                    squares(squares_for, lambda k: xT[:, k, 0:squares_for],
                            lambda k: act.wait_ge(x_new, base + k + 1))
                at.x_new += KT

            def quarter(n, last):
                for j in range(KT):
                    next_chunk()
                    bank = at.tile % 2
                    act.wait_ge(products, at.v("chunk", at.chunk))
                    nc.scalar.activation(tmpB[:, j % 2, 0:n], ps[:, bank, 0:n], ACT.Relu).then_inc(relu_ready, 1)
                    at.tile += 1
                    at.hidden += 1
                    act.wait_ge(relu_ready, at.v("hidden", at.hidden))
                    nc.scalar.activation(a_hi[:, j, 0:n], tmpB[:, j % 2, 0:n], ACT.Square).then_inc(hidden_hi, 1)
                for k in range(KT):
                    next_chunk()
                    if last:
                        act.wait_ge(tile_free[at.tile % 2], at.tile // 2 + 1)
                        if k >= 3:
                            act.wait_ge(sqacc_added, at.sqsum * (KT - 1) + k - 2)
                        dst = sqacc[:, 0:n] if k == 0 else tmpB[:, k % 2, 0:n]
                        nc.scalar.activation(dst, mix[:, k, 0:n], ACT.Square).then_inc(sq_ready, 1)
                        at.square += 1
                    at.tile += 1
                if last:
                    at.sqsum += 1

            def mlp(n):
                quarter(n, False)
                with act.Fori(0, QUARTERS - 2) as at.round:
                    quarter(n, False)
                at.rounds(QUARTERS - 2)
                quarter(n, True)

            for c in range(AHEAD):
                high_part(c)
            silu_c()
            act.wait_ge(x_in_ready, 16)
            squares(NTOK, lambda k: xT[:, k], lambda k: None)
            modulation(FIRST_GROUPS)
            for l in range(LAYERS):
                n = tokens(l)
                norm_in(l, NTOK, SH1)
                for b in range(3):
                    project(l, b)
                    attend(l, b)
                    merge(l, b)
                split_merged(n)
                project_out(n)
                norm_out(n, n)
                norm_in(l, n, SH2)
                mlp(n)
                norm_out(n, NTOK if l < LAYERS - 1 else 0)

        @block.vector
        def _(dve):
            at = Place()
            links = [0]

            def link(ins):
                links[0] += 1
                ins.then_inc(dve_link, 1)
                dve.wait_ge(dve_link, links[0])

            def setup():
                dve.wait_ge(small_in, 48)
                nc.vector.tensor_copy(idb[:], ident)
                nc.vector.tensor_copy(maskb[:].rearrange("p a b -> p (a b)"),
                                      const[:, C_MASK:C_MASK + 2 * P]).then_inc(tables, 1)
                dve.wait_ge(c_tanh, 1)
                link(nc.vector.scalar_tensor_tensor(out=c_silu[:], in0=c_t[:], scalar=1.0, in1=c_sb[:],
                                                    op0=ALU.add, op1=ALU.mult))
                nc.vector.tensor_scalar(c_silu[:], c_silu[:], 0.5, None, ALU.mult).then_inc(c_ready, 1)
                dve.wait_ge(c4_hi, 1)
                nc.vector.tensor_tensor(c4[:, :, 2:4], c_silu[:], c4[:, :, 0:2].bitcast(F32),
                                        ALU.subtract).then_inc(c4_ready, 1)
                for l in range(LAYERS):
                    v = vec[:, l, V_LAM:V_LAM + 4 * HEAD].rearrange("p (a b d) -> p a b d", a=2, b=2)
                    link(nc.vector.tensor_tensor(lam_t[:], v[:, :, 0], v[:, :, 1], ALU.mult))
                    link(nc.vector.reduce_sum(lam_s[:, 2 * l:2 * l + 2], lam_t[:], AX_X))
                nc.vector.tensor_scalar(lam_s[:], lam_s[:], 1.0, None, ALU.mult).then_inc(lam_ready, 1)
                dve.wait_ge(lam_exp, 1)
                for l in range(LAYERS):
                    lam_init = 0.8 - 0.6 * math.exp(-0.3 * l)
                    link(nc.vector.tensor_tensor(nlam[:, l:l + 1], lam_s[:, 2 * l + 1:2 * l + 2],
                                                 lam_s[:, 2 * l:2 * l + 1], ALU.subtract))
                    link(nc.vector.tensor_scalar(nlam[:, l:l + 1], nlam[:, l:l + 1], -lam_init, None, ALU.add))
                    link(nc.vector.tensor_scalar(gsub[:, l:l + 1], vec[:, l, V_GSUB:V_GSUB + 1], 1.0 - lam_init,
                                                 None, ALU.mult))
                    link(nc.vector.tensor_scalar(nsink[:, l], vec[:, l, V_SINK:V_SINK + 8], -1.0, None, ALU.mult))

            def add_squares(n, k):
                dve.wait_ge(sq_ready, at.square + k + 1)
                if k > 1:
                    dve.wait_ge(sqacc_added, at.sqsum * (KT - 1) + k - 1)
                nc.vector.tensor_tensor(sqacc[:, 0:n], sqacc[:, 0:n], tmpB[:, k % 2, 0:n],
                                        ALU.add).then_inc(sqacc_added, 1)
                if k == KT - 1:
                    at.square += KT
                    at.sqsum += 1

            def rstd(src, ncol, inv, eps, frees_out):
                v, nh, y, t = (stat[:, j, 0:ncol] for j in range(4))
                ins = nc.vector.tensor_scalar(v, src, inv, eps, ALU.mult, ALU.add)
                if frees_out:
                    ins.then_inc(out_free, 1)
                    at.out += 1
                    dve.wait_ge(out_free, at.out)
                else:
                    link(ins)
                nc.vector.tensor_scalar(nh, v, -0.5, None, ALU.mult)
                link(nc.vector.tensor_scalar(t.bitcast(I32), v.bitcast(I32), 1, None, ALU.logical_shift_right))
                link(nc.vector.tensor_scalar(y.bitcast(I32), t.bitcast(I32), -1.0, float(0x5F3759DF), ALU.mult,
                                             ALU.add))
                for j in range(3):
                    link(nc.vector.tensor_tensor(t, y, y, ALU.mult))
                    link(nc.vector.tensor_tensor(t, t, nh, ALU.mult))
                    ins = nc.vector.scalar_tensor_tensor(out=y, in0=t, scalar=1.5, in1=y, op0=ALU.add, op1=ALU.mult)
                    if j < 2:
                        link(ins)
                ins.then_inc(rstd_ready, 1)
                at.rstd += 1
                dve.wait_ge(rstd_ready, at.rstd)
                return y

            def rows(g, tile):
                dve.wait_ge(products, at.chunk)
                nc.vector.tensor_copy(ada_row[:, g % 2], ps[0:4, tile % 2]).then_inc(tile_free[tile % 2], 1)

            def columns(l, g):
                c = g * ADA_GROUP
                bank = at.tile % 2
                at.columns += 1
                dve.wait_ge(columns_done, at.columns)
                nc.vector.tensor_tensor(
                    ada[:, l, c:c + ADA_GROUP], ps[:, bank, 0:2 * ADA_GROUP].rearrange("p (c s) -> p c s", s=2),
                    vec[:, l, V_BADA + c:V_BADA + c + ADA_GROUP].unsqueeze(2).to_broadcast([P, ADA_GROUP, 2]),
                    ALU.add).then_inc(tile_free[bank], 1)
                at.tile += 1
                if g % 4 == 3:
                    dve.wait_ge(tile_free[bank], (at.tile - 1) // 2 + 1)
                    factors(l, g // 4)

            def factors(l, third):
                def gain(col):
                    return vec[:, l, col:col + KT].unsqueeze(2).to_broadcast([P, KT, 2])

                def pre(j, scale_at, col):
                    link(nc.vector.scalar_tensor_tensor(out=coef[:, l, j], in0=ada[:, l, scale_at:scale_at + KT],
                                                        scalar=1.0, in1=gain(col), op0=ALU.add, op1=ALU.mult))

                def post(j, gate_at, col):
                    link(nc.vector.tensor_tensor(coef[:, l, j], ada[:, l, gate_at:gate_at + KT], gain(col),
                                                 ALU.mult))

                if third == 0:
                    pre(0, SC1, V_GPRE1)
                elif third == 1:
                    post(1, GM1, V_GPOST1)
                else:
                    pre(2, SC2, V_GPRE2)
                    post(3, GM2, V_GPOST2)

            def modulation(l, groups):
                for g in range(groups):
                    at.chunk += ADA_GROUP
                    rows(g, at.tile)
                    at.tile += 1
                    if g:
                        columns(l, g - 1)
                columns(l, groups - 1)

            def token_rstd(n):
                dve.wait_ge(out_done, at.out + 1)
                rstd(ps[:, BANK_O, 0:n // P], n // P, 1.0 / D, EPS, True)
                dve.wait_ge(turn_done, at.turn + 1)

            def norm_in(l, n, which, shift_at):
                token_rstd(n)

                def scale(k):
                    if k >= 2:
                        dve.wait_ge(part_ready, at.part)
                    for s, a, z in halves(n):
                        ins = nc.vector.scalar_tensor_tensor(
                            out=tmpA[:, k % 2, a:z], in0=xT[:, k, a:z], scalar=coef[:, l, which, k, s:s + 1],
                            in1=ps[:, BANK_T, a:z], op0=ALU.mult, op1=ALU.mult)
                    ins.then_inc(scaled, 1)

                def low(k):
                    dve.wait_ge(part_hi, at.part + 1)
                    for s, a, z in halves(n):
                        ins = nc.vector.scalar_tensor_tensor(
                            out=h_lo[:, k, a:z], in0=tmpA[:, k % 2, a:z], scalar=ada[:, l, shift_at + k, s:s + 1],
                            in1=h_hi[:, k, a:z].bitcast(F32), op0=ALU.add, op1=ALU.subtract)
                    ins.then_inc(part_ready, 1)
                    at.part += 1

                for k in range(KT):
                    scale(k)
                    if k:
                        low(k - 1)
                low(KT - 1)
                at.scaled += KT
                dve.wait_ge(scaled, at.scaled)
                dve.sem_inc(turn_free, 1)
                at.turn += 1

            def norm_out(l, n, which, squares_for):
                token_rstd(n)
                for k in range(KT):
                    for s, a, z in halves(n):
                        ins = nc.vector.scalar_tensor_tensor(
                            out=tmpA[:, k % 2, a:z], in0=mix[:, k, a:z], scalar=coef[:, l, which, k, s:s + 1],
                            in1=ps[:, BANK_T, a:z], op0=ALU.mult, op1=ALU.mult)
                    if k == KT - 1:
                        ins.then_inc(turn_free, 1)
                        at.turn += 1
                        dve.wait_ge(turn_free, at.turn)
                    else:
                        link(ins)
                    nc.vector.tensor_tensor(xT[:, k, 0:n], xT[:, k, 0:n], tmpA[:, k % 2, 0:n],
                                            ALU.add).then_inc(x_new, 1)
                    if squares_for and k > 1:
                        add_squares(squares_for, k - 1)
                if squares_for:
                    add_squares(squares_for, KT - 1)

            def rope(dst):
                x = dst[:, 0:NX]
                if at.roped:
                    dve.wait_ge(roped, at.roped)
                link(nc.vector.stream_shuffle(shuf[:], x, [(j + 16) % 32 for j in range(32)]))
                nc.vector.tensor_tensor(x, x, cos, ALU.mult)
                link(nc.vector.tensor_tensor(shuf[:], shuf[:], sin, ALU.mult))
                nc.vector.tensor_tensor(x, x, shuf[:], ALU.add).then_inc(roped, 1)
                at.roped += 1

            def project(l, b):
                n = tokens(l)
                if b == 1:
                    nc.vector.memset(v_sb[:, :, HEAD:2 * HEAD], 0.0).then_inc(zeroed, 1)
                at.chunk += len(PROJ[b])
                for kind, t in PROJ[b]:
                    if kind == "v":
                        at.turn += 1
                    elif b != 1:
                        dve.wait_ge(tile_free[at.tile % 2], at.tile // 2 + 1)
                        rope({"q": q_sb, "k": k_sb}[kind][:, t])
                    at.tile += 1
                if b != 1:
                    return
                tiles = [(k_sb, 0, NTOK, V_GK)] + [(q_sb, t, n, V_GQ) for t in range(4)]
                starts = [0]
                for _, _, m, _ in tiles:
                    starts.append(starts[-1] + 2 * m // P)
                dve.wait_ge(out_done, at.out + 1)
                y = rstd(ps[:, BANK_O, 0:starts[-1]], starts[-1], 1.0 / HEAD, EPS, True)

                def expand(j):
                    tt = tiles[j][2] // P
                    src = y[:, starts[j]:starts[j + 1]].rearrange("p (t h) -> p t h", h=2)
                    nc.vector.tensor_copy(tmpA[:, j % 2, 0:tt * P].rearrange("p (t h d) -> p t h d", t=tt, h=2),
                                          src.unsqueeze(3).to_broadcast([P, tt, 2, HEAD])).then_inc(spread, 1)

                def finish(j):
                    buf, t, m, col = tiles[j]
                    dve.wait_ge(turn_done, at.turn + 1)
                    nc.vector.scalar_tensor_tensor(out=buf[:, t, 0:m], in0=buf[:, t, 0:m],
                                                   scalar=vec[:, l, col:col + 1], in1=ps[:, BANK_T, 0:m],
                                                   op0=ALU.mult, op1=ALU.mult).then_inc(turn_free, 1)
                    at.turn += 1
                    dve.wait_ge(turn_free, at.turn)
                    rope(buf[:, t])

                expand(0)
                expand(1)
                finish(0)
                finish(1)
                return expand, finish

            def attend(l, b, head_norm):
                todo = units(l)
                per = n_items(b)
                n = tokens(l)

                def bounds(i):
                    t, qt = todo[i]
                    a, z = keys(qt)
                    slot = at.unit % 2
                    for m in range(2):
                        dve.wait_ge(scores_done, at.map + 1)
                        nc.vector.reduce_max(mx[:, slot, m:m + 1], ps[:, BANK_S + at.map % 4, a:z],
                                             AX_X).then_inc(max_done, 1)
                        at.map += 1
                    dve.wait_ge(max_done, at.map)
                    if b == 2:
                        nc.vector.scalar_tensor_tensor(
                            out=negm[:, slot], in0=mx[:, slot], scalar=-SCALE, in1=nsink[:, l, 2 * t:2 * t + 2],
                            op0=ALU.mult, op1=ALU.min).then_inc(bound_ready, 1)
                        dve.wait_ge(bound_ready, at.unit + 1)
                        nc.vector.tensor_tensor(dsink[:, slot], negm[:, slot], nsink[:, l, 2 * t:2 * t + 2],
                                                ALU.subtract).then_inc(dsink_ready, 1)
                    else:
                        nc.vector.tensor_scalar(negm[:, slot], mx[:, slot], -SCALE, None,
                                                ALU.mult).then_inc(bound_ready, 1)
                    at.unit += 1

                def normalise(i):
                    t, qt = todo[i]
                    a, z = keys(qt)
                    slot = at.item % 2
                    dve.wait_ge(exp_done, 2 * (at.item + 1))
                    if b == 2:
                        dve.wait_ge(esink_ready, at.gate + 1)
                        at.gate += 1
                        link(nc.vector.tensor_tensor(sums[:, slot], sums[:, slot], esink[:, slot], ALU.add))
                    link(nc.vector.reciprocal(rsum[:, slot], sums[:, slot]))
                    e = [prob[:, slot, m, a:z] for m in range(2)]
                    if b == 0:
                        link(nc.vector.tensor_scalar(rsum[:, slot, 1:2], rsum[:, slot, 1:2], nlam[:, l:l + 1], None,
                                                     ALU.mult))
                        link(nc.vector.tensor_scalar(e[0], e[0], rsum[:, slot, 0:1], None, ALU.mult))
                        nc.vector.scalar_tensor_tensor(out=e[0], in0=e[1], scalar=rsum[:, slot, 1:2], in1=e[0],
                                                       op0=ALU.mult, op1=ALU.add).then_inc(probs_ready, 1)
                    else:
                        for m in range(2):
                            nc.vector.tensor_scalar(e[m], e[m], rsum[:, slot, m:m + 1], None,
                                                    ALU.mult).then_inc(probs_ready, 1)
                    at.item += 1

                def output(i):
                    t, qt = todo[i]
                    at.split += 1
                    dve.wait_ge(out_hi, at.split)
                    cols = slice(qt * P, (qt + 1) * P)
                    nc.vector.tensor_tensor(a_lo[:, t, cols], ps[:, BANK_O, 0:P], a_hi[:, t, cols].bitcast(F32),
                                            ALU.subtract).then_inc(out_free, 1)

                fill_l, group, end, chunks = FILL[l, b]
                filled, ready, tile = 0, None, None
                bounds(0)
                for i, (t, qt) in enumerate(todo):
                    normalise(i)
                    if i + 1 < len(todo):
                        bounds(i + 1)
                    if b and i >= 1:
                        output(i - 1)
                    at.turn += per
                    if b == 1 and qt == 0 and t < 3:
                        expand, finish = head_norm
                        expand(t + 2)
                        finish(t + 2)
                    for _ in range(chunks):
                        if filled % ADA_GROUP == 0:
                            tile = at.tile
                            at.tile += 1
                        at.chunk += 1
                        filled += 1
                        if filled % ADA_GROUP == 2 and ready is not None:
                            columns(fill_l, ready)
                            ready = None
                        if filled % ADA_GROUP == 0:
                            rows(group, tile)
                            ready = group
                            group += 1
                if b:
                    output(len(todo) - 1)
                columns(fill_l, ready)
                at.out += len(todo)
                if b == 0:
                    at.araw += len(todo)
                    dve.wait_ge(a_squares, at.araw)
                    y = rstd(ssA[:, 0:len(todo)], len(todo), 1.0 / P, SUBLN_EPS, False)
                    for i, (t, qt) in enumerate(todo):
                        dst = mix[:, qt, t * P:(t + 1) * P]
                        nc.vector.tensor_scalar(dst, dst, y[:, i:i + 1], None, ALU.mult).then_inc(a_scaled, 1)
                    for t in range(4):
                        at.split += 1
                        dve.wait_ge(out_hi, at.split)
                        nc.vector.scalar_tensor_tensor(
                            out=a_lo[:, t, 0:n], in0=ps[:, BANK_T, 0:n], scalar=gsub[:, l:l + 1],
                            in1=a_hi[:, t, 0:n].bitcast(F32), op0=ALU.mult, op1=ALU.subtract).then_inc(turn_free, 1)
                        at.turn += 1

            def merge(l, b):
                n = tokens(l)
                for pair in range(KT // 2):
                    gates = at.tile
                    at.tile += 2
                    at.chunk += 3
                    for j in range(2):
                        k = 2 * pair + j
                        dve.wait_ge(tile_free[(gates + j) % 2], (gates + j) // 2 + 1)
                        if j == 0:
                            at.half += 1
                            dve.wait_ge(half_products, at.half)
                        else:
                            dve.wait_ge(products, at.chunk)
                        dst = mix[:, k, 0:n] if b == 0 else tmpA[:, j, 0:n]
                        bank = at.tile % 2
                        nc.vector.scalar_tensor_tensor(
                            out=dst, in0=tmpB[:, j, 0:n], scalar=1.0, in1=ps[:, bank, 0:n],
                            op0=ALU.add, op1=ALU.mult).then_inc(tile_free[bank], 1)
                        if b:
                            dve.wait_ge(tile_free[bank], at.tile // 2 + 1)
                            ins = nc.vector.tensor_tensor(mix[:, k, 0:n], mix[:, k, 0:n], tmpA[:, j, 0:n], ALU.add)
                            if b == 1:
                                link(ins)
                            else:
                                ins.then_inc(merged, 1)
                        at.tile += 1

            def split_merged(n):
                for k in range(KT):
                    dve.wait_ge(part_hi, at.part + 1)
                    ins = nc.vector.scalar_tensor_tensor(
                        out=h_lo[:, k, 0:n], in0=mix[:, k, 0:n], scalar=0.5, in1=h_hi[:, k, 0:n].bitcast(F32),
                        op0=ALU.mult, op1=ALU.subtract)
                    ins.then_inc(part_ready, 1)
                    at.part += 1

            def project_out(n):
                at.chunk += KT
                for k in range(KT):
                    bank = at.tile % 2
                    dve.wait_ge(sq_ready, at.square + k + 1)
                    nc.vector.tensor_copy(mix[:, k, 0:n], ps[:, bank, 0:n]).then_inc(tile_free[bank], 1)
                    at.tile += 1
                    if 1 <= k < KT - 1:
                        add_squares(n, k)
                add_squares(n, KT - 1)

            def quarter(n, last):
                for j in range(KT):
                    bank = at.tile % 2
                    at.hidden += 1
                    dve.wait_ge(relu_ready, at.v("hidden", at.hidden))
                    nc.vector.scalar_tensor_tensor(out=tmpA[:, j % 2, 0:n], in0=ps[:, bank, 0:n], scalar=0.0,
                                                   in1=tmpB[:, j % 2, 0:n], op0=ALU.max,
                                                   op1=ALU.mult).then_inc(tile_free[bank], 1)
                    dve.wait_ge(tile_free[bank], at.v("bank", at.tile // 2 + 1))
                    dve.wait_ge(hidden_hi, at.v("hidden", at.hidden))
                    nc.vector.tensor_tensor(a_lo[:, j, 0:n], tmpA[:, j % 2, 0:n], a_hi[:, j, 0:n].bitcast(F32),
                                            ALU.subtract).then_inc(hidden_ready, 1)
                    at.tile += 1
                at.chunk += KT
                for k in range(KT):
                    bank = at.tile % 2
                    at.chunk += 1
                    dve.wait_ge(products, at.v("chunk", at.chunk))
                    nc.vector.tensor_tensor(mix[:, k, 0:n], mix[:, k, 0:n], ps[:, bank, 0:n],
                                            ALU.add).then_inc(tile_free[bank], 1)
                    at.tile += 1
                    if last and k > 1:
                        add_squares(n, k - 1)
                if last:
                    add_squares(n, KT - 1)

            def mlp(n):
                link(nc.vector.memset(mix[:, :, 0:n], 0.0))
                quarter(n, False)
                with dve.Fori(0, QUARTERS - 2) as at.round:
                    quarter(n, False)
                at.rounds(QUARTERS - 2)
                quarter(n, True)

            setup()
            for k in range(1, KT):
                add_squares(NTOK, k)
            modulation(0, FIRST_GROUPS)
            for l in range(LAYERS):
                n = tokens(l)
                norm_in(l, NTOK, 0, SH1)
                for b in range(3):
                    attend(l, b, project(l, b))
                    merge(l, b)
                split_merged(n)
                project_out(n)
                norm_out(l, n, 1, n)
                norm_in(l, n, 2, SH2)
                mlp(n)
                norm_out(l, n, 3, NTOK if l < LAYERS - 1 else 0)

        @block.tensor
        def _(pe):
            at = Place()

            def blocks(bank, jobs, hi, lo, n, ready=None):
                slot = at.chunk % SLOTS
                for i, (blk, k) in enumerate(jobs):
                    if ready:
                        ready(k)
                    cols = slice(blk * P, (blk + 1) * P)
                    for p, (w, a) in enumerate(((w_hi, hi), (w_lo, hi), (w_hi, lo))):
                        ins = nc.tensor.matmul(ps[:, bank, 0:n], w[:, slot, cols], a[:, k, 0:n],
                                               start=(i == 0 and p == 0), stop=(i == len(jobs) - 1 and p == 2))
                return ins

            def chunk_wait():
                pe.wait_ge(lo_ready, at.v("chunk", at.chunk + 1))

            def open_tile():
                bank = at.tile % 2
                if at.tile >= 2:
                    pe.wait_ge(tile_free[bank], at.v("bank", at.tile // 2))
                at.tile += 1
                return bank

            def product_pair(hi, lo, n, ready):
                banks = [open_tile(), open_tile()]
                pe.wait_ge(lo_ready, at.v("chunk", at.chunk + 2))
                for k in range(KT):
                    ready(k)
                    for j, bank in enumerate(banks):
                        slot = (at.chunk + j) % SLOTS
                        cols = slice(k * P, (k + 1) * P)
                        for p, (w, a) in enumerate(((w_hi, hi), (w_lo, hi), (w_hi, lo))):
                            ins = nc.tensor.matmul(ps[:, bank, 0:n], w[:, slot, cols], a[:, k, 0:n],
                                                   start=(k == 0 and p == 0), stop=(k == KT - 1 and p == 2))
                        if k == KT - 1:
                            ins.then_inc(products, 1)
                at.chunk += 2

            def product(hi, lo, n, ready=None):
                chunk_wait()
                blocks(open_tile(), [(k, k) for k in range(KT)], hi, lo, n, ready).then_inc(products, 1)
                at.chunk += 1

            def open_turn():
                if at.turn:
                    pe.wait_ge(turn_free, at.turn)
                at.turn += 1

            def open_out():
                if at.out:
                    pe.wait_ge(out_free, at.out)
                at.out += 1

            def turn(tiles):
                for src, col in tiles:
                    ins = nc.tensor.transpose(ps[:, BANK_T, col:col + P], src, ident)
                ins.then_inc(turn_done, 1)

            def row_chunk(j, bank):
                chunk_wait()
                slot = at.chunk % SLOTS
                for k in range(KT):
                    for w in (w_hi, w_lo):
                        ins = nc.tensor.matmul(ps[0:4, bank, j * P:(j + 1) * P], c4[:, k],
                                               w[:, slot, k * P:(k + 1) * P],
                                               start=(k == 0 and w is w_hi), stop=(k == KT - 1 and w is w_lo))
                ins.then_inc(products, 1)
                at.chunk += 1

            def columns(g, tile):
                pe.wait_ge(tile_free[tile % 2], tile // 2 + 1)
                bank = open_tile()
                for j in range(ADA_GROUP):
                    ins = nc.tensor.matmul(ps[:, bank, 2 * j:2 * j + 2], ada_row[:, g % 2, j * P:(j + 1) * P],
                                           comb, start=True, stop=True)
                ins.then_inc(columns_done, 1)

            def modulation(groups):
                before = None
                for g in range(groups):
                    tile = at.tile
                    bank = open_tile()
                    for j in range(ADA_GROUP):
                        row_chunk(j, bank)
                    if before:
                        columns(*before)
                    before = (g, tile)
                columns(*before)

            def token_rstd(n):
                at.sqsum += 1
                pe.wait_ge(sqacc_added, at.sqsum * (KT - 1))
                open_out()
                for t in range(n // P):
                    ins = nc.tensor.matmul(ps[:, BANK_O, t:t + 1], sqacc[:, t * P:(t + 1) * P], ones,
                                           start=True, stop=True)
                ins.then_inc(out_done, 1)
                at.rstd += 1
                pe.wait_ge(rstd_ready, at.rstd)
                open_turn()
                turn([(stat[:, 2, t:t + 1].to_broadcast([P, P]), t * P) for t in range(n // P)])

            def next_part(k):
                at.part += 1
                pe.wait_ge(part_ready, at.part)

            def project(l, b):
                n = tokens(l)
                pending = None
                heads_at = of_b = 0

                def turn_values(t, bank, tile):
                    pe.wait_ge(tile_free[bank], tile // 2 + 1)
                    open_turn()
                    turn([(prob[:, 0, t % 2, j * P:(j + 1) * P], j * P) for j in range(NTOK // P)])

                def head_sums(m):
                    nonlocal heads_at, of_b
                    if heads_at == 0:
                        open_out()
                    at.hsq += 1
                    pe.wait_ge(head_sq, at.hsq)
                    for j in range(m // P):
                        ins = nc.tensor.matmul(ps[:, BANK_O, heads_at:heads_at + 2],
                                               tmpB[:, of_b % 2, j * P:(j + 1) * P], heads,
                                               start=True, stop=True)
                        heads_at += 2
                    of_b += 1
                    ins.then_inc(out_done if of_b == len(PROJ[1]) - 1 else head_summed, 1)

                for i, (kind, t) in enumerate(PROJ[b]):
                    tile = at.tile
                    if b == 0 and i == 0:
                        product_pair(h_hi, h_lo, NTOK, next_part)
                        turn_values(t, tile % 2, tile)
                        continue
                    if b == 0 and i == 1:
                        tile -= 1
                    else:
                        product(h_hi, h_lo, n if kind == "q" else NTOK)
                    if pending:
                        pending()
                    pending = None
                    if kind == "v":
                        pending = lambda t=t, tile=tile: turn_values(t, tile % 2, tile)
                    elif b == 1:
                        pending = lambda m=n if kind == "q" else NTOK: head_sums(m)
                if pending:
                    pending()
                if b == 1:
                    at.rstd += 1
                    pe.wait_ge(rstd_ready, at.rstd)
                    spread_heads(0, NTOK)
                    spread_heads(1, n)

            def spread_heads(j, m):
                at.spread += 1
                pe.wait_ge(spread, at.spread)
                open_turn()
                turn([(tmpA[:, j % 2, i * P:(i + 1) * P], i * P) for i in range(m // P)])

            def attend(l, b):
                todo = units(l)
                per = n_items(b)
                roped_before = at.roped
                first_q = sum(kind == "k" for kind, _ in PROJ[b])
                at.roped += first_q + 4

                def scores(i):
                    t, qt = todo[i]
                    a, z = keys(qt)
                    kt = t if b == 0 else 0
                    pe.wait_ge(roped, roped_before + first_q + t + 1)
                    window = b == 2 and qt < NX // P
                    for m in range(2):
                        rows = slice(m * HEAD, (m + 1) * HEAD)
                        if at.map >= 4:
                            pe.wait_ge(exp_done, at.map - 3)
                        bank = BANK_S + at.map % 4
                        ins = nc.tensor.matmul(ps[:, bank, a:z], q_sb[rows, t, qt * P:(qt + 1) * P],
                                               k_sb[rows, kt, a:z], start=True, stop=not window)
                        if window:
                            other = (1 - qt) * P
                            ins = nc.tensor.matmul(ps[:, bank, other:other + P], idb[:], maskb[:, qt],
                                                   start=False, stop=True)
                        ins.then_inc(scores_done, 1)
                        at.map += 1

                def turn_probs(i, m):
                    t, qt = todo[i]
                    a, z = keys(qt)
                    at.item += 1
                    pe.wait_ge(probs_ready, at.item)
                    open_turn()
                    turn([(prob[:, (at.unit + i) % 2, m, c:c + P], c) for c in range(a, z, P)])
                    return at.turn - 1, (at.item - 1) % 2

                def weigh(i, m, event, slot):
                    t, qt = todo[i]
                    a, z = keys(qt)
                    pe.wait_ge(turn_free, event + 1)
                    if m == 0:
                        open_out()
                    for c in range(a, z, P):
                        pT = probT[:, slot, c:c + P]
                        if b == 0:
                            v = v_sb[:, c // P, t * P:(t + 1) * P]
                            lhs, rhs = pT, v
                        else:
                            lhs, rhs = v_sb[:, c // P, m * HEAD:m * HEAD + P], pT
                        ins = nc.tensor.matmul(ps[:, BANK_O, 0:P], lhs, rhs, start=(c == a and m == 0),
                                               stop=(c == z - P and m == per - 1))
                    if m == per - 1:
                        ins.then_inc(out_done, 1)

                if b == 1:
                    pe.wait_ge(zeroed, l + 1)
                if b == 2 and l == 0:
                    pe.wait_ge(tables, 1)
                scores(0)
                before = None
                _, group, end, chunks = FILL[l, b]
                filled, ready, tile = 0, None, None
                for i, (t, qt) in enumerate(todo):
                    if i + 1 < len(todo):
                        scores(i + 1)
                    for _ in range(chunks):
                        if filled % ADA_GROUP == 0:
                            tile = at.tile
                            bank = open_tile()
                        row_chunk(filled % ADA_GROUP, bank)
                        filled += 1
                        if filled % ADA_GROUP == 2 and ready is not None:
                            columns(*ready)
                            ready = None
                        if filled % ADA_GROUP == 0:
                            ready = (group, tile)
                            group += 1
                    for m in range(per):
                        event, slot = turn_probs(i, m)
                        if before:
                            weigh(*before)
                        before = (i, m, event, slot)
                    if b == 1 and qt == 0 and t < 3:
                        spread_heads(t + 2, tokens(l))
                weigh(*before)
                columns(*ready)
                at.unit += len(todo)
                if b == 0:
                    at.rstd += 1

            def turn_a(l):
                ntt = tokens(l) // P
                for t in range(4):
                    at.scaled += ntt
                    pe.wait_ge(a_scaled, at.scaled)
                    open_turn()
                    turn([(mix[:, j, t * P:(t + 1) * P], j * P) for j in range(ntt)])

            def merge(l, b):
                n = tokens(l)
                for pair in range(KT // 2):
                    product(h_hi, h_lo, n)
                    product(h_hi, h_lo, n)
                    if pair == 0:
                        if b == 0:
                            turn_a(l)
                        pe.wait_ge(turn_free, at.turn)
                        pe.wait_ge(out_free, at.out)
                    chunk_wait()
                    for j in range(2):
                        blocks(open_tile(), [(4 * j + i, i) for i in range(4)], a_hi, a_lo, n
                               ).then_inc(products if j else half_products, 1)
                    at.chunk += 1

            def project_out(n):
                product_pair(h_hi, h_lo, n, next_part)
                for _ in range(2, KT):
                    product(h_hi, h_lo, n)

            def quarter(n, first):
                if first:
                    product_pair(h_hi, h_lo, n, next_part)
                for _ in range(2 if first else 0, KT):
                    product(h_hi, h_lo, n)

                def next_hidden(k):
                    at.hidden += 1
                    pe.wait_ge(hidden_ready, at.v("hidden", at.hidden))

                for k in range(KT):
                    product(a_hi, a_lo, n, next_hidden if k == 0 else None)

            def mlp(n):
                quarter(n, True)
                with pe.Fori(0, QUARTERS - 2) as at.round:
                    quarter(n, False)
                at.rounds(QUARTERS - 2)
                quarter(n, False)

            pe.wait_ge(small_in, 48)
            pe.wait_ge(c4_ready, 1)
            modulation(FIRST_GROUPS)
            for l in range(LAYERS):
                n = tokens(l)
                token_rstd(NTOK)
                for b in range(3):
                    project(l, b)
                    attend(l, b)
                    merge(l, b)
                project_out(n)
                token_rstd(n)
                token_rstd(n)
                mlp(n)
                token_rstd(n)


def arrange(inputs):
    def blocks(w):
        return w.reshape(-1, P, P).transpose(1, 0, 2).reshape(P, -1)

    def pair_heads(a, axis):
        a = np.moveaxis(a, axis, 0)
        a = a.reshape((2, 4, HEAD) + a.shape[1:]).swapaxes(0, 1).reshape(a.shape)
        return np.moveaxis(a, 0, axis)

    chunks, vecs = [], []
    for l in range(LAYERS):
        w_in, w_branch = inputs["w_in"][l], inputs["w_branch"][l]
        w_out, w1, w2 = inputs["w_out"][l], inputs["w_ff1"][l], inputs["w_ff2"][l]
        cols = lambda w, j: w[:, j * P:(j + 1) * P]
        ada_chunks = lambda layer, first, end: [blocks(cols(inputs["w_ada"][layer], j))
                                                for j in range(first * ADA_GROUP, end * ADA_GROUP)]
        if l == 0:
            chunks += ada_chunks(0, 0, FIRST_GROUPS)
        widths = dict(qa=512, ka=512, va=512, qb=512, kb=P, vb=P, qc=512, kc=P, vc=P, gt=3 * D)
        part, start = {}, 0
        for name, width in widths.items():
            part[name] = w_in[:, start:start + width]
            start += width
        for b, name in enumerate("abc"):
            if b:
                part["q" + name] = pair_heads(part["q" + name], 1)
            wb = w_branch[b * 512:(b + 1) * 512]
            if b:
                wb = pair_heads(wb, 0)
            chunks += [blocks(cols(part[kind + name], t)) for kind, t in PROJ[b]]
            chunks += ada_chunks(*FILL[l, b][:3])
            for pair in range(KT // 2):
                chunks += [blocks(cols(part["gt"], b * KT + 2 * pair + j)) for j in range(2)]
                chunks.append(np.concatenate([blocks(cols(wb, 2 * pair + j)) for j in range(2)], 1))
        chunks += [blocks(cols(w_out, j)) for j in range(KT)]
        for r in range(QUARTERS):
            chunks += [blocks(cols(w1, r * KT + j)) for j in range(KT)]
            chunks += [blocks(cols(w2[r * D:(r + 1) * D], j)) for j in range(KT)]
        v = np.zeros((P, NV), np.float32)
        v[:, V_BADA:V_BADA + ADA_CHUNKS] = inputs["b_ada"][l].reshape(-1, P).T
        for col, name in ((V_GPRE1, "g_pre_mix"), (V_GPOST1, "g_post_mix"), (V_GPRE2, "g_pre_ff"),
                          (V_GPOST2, "g_post_ff")):
            v[:, col:col + KT] = inputs[name][l].reshape(KT, P).T
        v[:, V_GQ] = np.tile(inputs["g_qnorm"][l], 2)
        v[:, V_GK] = np.tile(inputs["g_knorm"][l], 2)
        v[:, V_GSUB] = inputs["g_subln"][l]
        v[:, V_SINK:V_SINK + 8] = inputs["sink"][l].reshape(2, 4).T.reshape(1, 8)
        for j, name in enumerate(("lam_q1", "lam_k1", "lam_q2", "lam_k2")):
            v[:, V_LAM + j * HEAD:V_LAM + (j + 1) * HEAD] = inputs[name][l][None]
        vecs.append(v)
    feature_major = lambda a: a.reshape(-1, KT, P).transpose(2, 1, 0)
    x = np.concatenate([inputs["x"][0], inputs["ctx"][0]], 0)
    c = np.concatenate([inputs["c"], inputs["c_ctx"][None]], 0)
    return {
        "x_in": np.ascontiguousarray(feature_major(x)),
        "w_all": np.stack(chunks),
        "vec_in": np.ascontiguousarray(np.stack(vecs, 1)),
        "c_in": np.ascontiguousarray(feature_major(c)),
        "const_in": shape_constants(),
    }


def kernel(**inputs):
    import concourse.bacc as bacc
    from concourse.bass_utils import run_bass_kernel_spmd

    arrays = arrange({k: np.asarray(v) for k, v in inputs.items()})
    nc = bacc.Bacc("TRN2", target_bir_lowering=False, num_devices=1)
    args = [nc.dram_tensor(name, a.shape, F32, kind="ExternalInput").ap() for name, a in arrays.items()]
    args.append(nc.dram_tensor("out", (P, KT, NX), F32, kind="ExternalOutput").ap())
    build_trunk(nc, *args)
    r = run_bass_kernel_spmd(nc, [arrays], core_ids=[0])
    return r.results[0]["out"].transpose(2, 1, 0).reshape(1, NX, D)
```

```python
import math
from contextlib import ExitStack

import numpy as np

import concourse.bass as bass
from concourse import mybir

F32 = mybir.dt.float32
F32R = mybir.dt.float32r
BF16 = mybir.dt.bfloat16
I32 = mybir.dt.int32
ALU = mybir.AluOpType
ACT = mybir.ActivationFunctionType
AX_X = mybir.AxisListType.X

P = 128
D = 1024
KT = D // P
NX, NY = 256, 256
NTOK = NX + NY
LAYERS = 2
D_FF = 4096
HEAD = 64
GRID_W = 64
ROPE_THETA = 10000.0
EPS = 1e-6
SUBLN_EPS = 1e-5
SCALE = HEAD ** -0.5
MASKED = -1e30

CW = KT * P
SLOTS = 4
ADA_CHUNKS = 6 * KT
ADA_GROUP = 4
PROJ = {0: [("v", 0), ("v", 1), ("v", 2), ("v", 3), ("k", 0), ("k", 1), ("k", 2), ("k", 3),
            ("q", 0), ("q", 1), ("q", 2), ("q", 3)],
        1: [("k", 0), ("q", 0), ("v", 0), ("q", 1), ("q", 2), ("q", 3)],
        2: [("v", 0), ("k", 0), ("q", 0), ("q", 1), ("q", 2), ("q", 3)]}
FIRST = [(0, g) for g in range(4)]
FILL = {(0, 0): [(0, 4), (0, 5), (0, 6)], (0, 1): [(0, 7), (0, 8), (0, 9), (1, 0)], (0, 2): [(1, 1), (1, 2), (1, 3)],
        (1, 0): [(1, 6), (1, 7)], (1, 1): [(1, 8), (1, 9)], (1, 2): []}
MIDDLE = {0: [(0, 10), (0, 11)], 1: [(1, 10), (1, 11)]}
BETWEEN = {0: [(1, 4), (1, 5)]}
DIRECT = len(FIRST) * ADA_GROUP
QUARTERS = D_FF // D
CHUNKS_OF_LAYER = ADA_CHUNKS + sum(map(len, PROJ.values())) + 3 * (KT + KT // 2) + KT + 2 * QUARTERS * KT
NCHUNK = LAYERS * CHUNKS_OF_LAYER
AHEAD = 3

V_BADA = 0
V_GPRE1 = 48
V_GPOST1 = 56
V_GPRE2 = 64
V_GPOST2 = 72
V_GQ = 80
V_GK = 81
V_GSUB = 82
V_SINK = 83
V_LAM = 91
NV = V_LAM + 4 * HEAD
C_COS = 0
C_SIN = C_COS + NX
C_ID = C_SIN + NX
C_MASK = C_ID + P
C_HEADS = C_MASK + 2 * P
C_ONE = C_HEADS + 2
NC = C_ONE + 1


def shape_constants():
    t = np.arange(NX)
    half = HEAD // 2
    inv = np.power(np.float32(ROPE_THETA), -np.arange(0, half, 2, dtype=np.float32) / np.float32(half))
    row = (t // GRID_W).astype(np.float32)
    col = (t % GRID_W).astype(np.float32)
    cos = np.zeros((P, NX), np.float32)
    sin = np.zeros((P, NX), np.float32)
    for p in range(P):
        d = p % HEAD
        pos = row if d < half else col
        ang = (pos * inv[d % (half // 2)]).astype(np.float32)
        cos[p] = np.cos(ang)
        sin[p] = np.sin(ang) * (-1.0 if d % half < half // 2 else 1.0)
    c = np.zeros((P, NC), np.float32)
    c[:, C_COS:C_COS + NX] = cos
    c[:, C_SIN:C_SIN + NX] = sin
    c[:, C_ID:C_ID + P] = np.eye(P)
    q, k = np.arange(P)[:, None], np.arange(P)[None, :]
    c[:, C_MASK:C_MASK + P] = np.where(k > q, MASKED, 0.0)
    c[:, C_MASK + P:C_MASK + 2 * P] = np.where(k < q, MASKED, 0.0)
    c[:HEAD, C_HEADS] = 1.0
    c[HEAD:, C_HEADS + 1] = 1.0
    c[:, C_ONE] = 1.0
    return c


class Place:
    PER_ROUND = {"chunk": 2 * KT, "raw": 16 * 2 * KT // SLOTS, "bank": KT, "hidden": KT}

    def __init__(self):
        self.chunk = self.tile = self.turn = self.out = self.map = self.item = self.unit = 0
        self.roped = self.rstd = self.square = self.part = self.x_new = self.sqsum = self.hsq = 0
        self.gate = self.spread = self.hidden = self.split = self.araw = self.scaled = self.merged = self.half = 0
        self.out_scaled = self.columns = self.qk = self.diff = 0
        self.round = None
        self.last_tile = None

    def v(self, kind, n):
        return n if self.round is None else self.round * self.PER_ROUND[kind] + n

    def rounds(self, n):
        self.round = None
        self.chunk += (n - 1) * 2 * KT
        self.tile += (n - 1) * 2 * KT
        self.hidden += (n - 1) * KT


def finish(steps):
    for _ in steps:
        pass


def build_trunk(nc, x_in, w_all, vec_in, c_in, const_in, out):
    with ExitStack() as ctx:
        def sb(name, shape, dt=F32):
            return ctx.enter_context(nc.sbuf_tensor(name, shape, dt))

        def sem(name):
            return ctx.enter_context(nc.semaphore(name))

        ps = ctx.enter_context(nc.psum_tensor("ps", [P, 8, 512], F32))
        BANK_S, BANK_T, BANK_O = 2, 6, 7

        raw = sb("raw", [P, SLOTS, CW])
        w_hi = sb("w_hi", [P, SLOTS, CW], F32R)
        w_lo = sb("w_lo", [P, SLOTS, CW], F32R)
        xT = sb("xT", [P, KT, NTOK])
        h_hi = sb("h_hi", [P, KT, NTOK], F32R)
        h_lo = sb("h_lo", [P, KT, NTOK], F32R)
        a_hi = sb("a_hi", [P, KT, NTOK], F32R)
        a_lo = sb("a_lo", [P, KT, NTOK], F32R)
        mix = sb("mix", [P, KT, NTOK])
        k_hi = sb("k_hi", [P, 4, NTOK], F32R)
        k_lo = sb("k_lo", [P, 4, NTOK], F32R)
        v_sb = sb("v_sb", [P, 4, 4 * P])
        prob = sb("prob", [P, 2, 2, 512])
        probT = sb("probT", [P, 2, 512])
        tmpA = sb("tmpA", [P, 2, 512])
        tmpB = sb("tmpB", [P, 2, 512])
        sqacc = sb("sqacc", [P, 512])
        shuf = sb("shuf", [P, NX])
        ada_row = sb("ada_row", [4, 2, 512])
        const = sb("const", [P, NC])
        idb = sb("idb", [P, P], BF16)
        maskb = sb("maskb", [P, 2, P], BF16)
        vec = sb("vec", [P, LAYERS, NV])
        c_sb = sb("c_sb", [P, KT, 2])
        c_t = sb("c_t", [P, KT, 2])
        c_silu = sb("c_silu", [P, KT, 2])
        c4 = sb("c4", [P, KT, 4], F32R)
        ada = sb("ada", [P, LAYERS, ADA_CHUNKS, 2])
        coef = sb("coef", [P, LAYERS, 4, KT, 2])
        stat = sb("stat", [P, 4, 48])
        lam_t = sb("lam_t", [P, 2, HEAD])
        lam_s = sb("lam_s", [P, 4])
        nlam = sb("nlam", [P, LAYERS])
        gsub = sb("gsub", [P, LAYERS])
        nsink = sb("nsink", [P, LAYERS, 8])
        mx = sb("mx", [P, 2, 2])
        negm = sb("negm", [P, 2, 2])
        sums = sb("sums", [P, 2, 2])
        esink = sb("esink", [P, 2, 2])
        dsink = sb("dsink", [P, 2, 2])
        rsum = sb("rsum", [P, 2, 2])
        ssA = sb("ssA", [P, 16])

        ident = const[:, C_ID:C_ID + P]
        cos = const[:, C_COS:C_COS + NX]
        sin = const[:, C_SIN:C_SIN + NX]
        ones = const[:, C_ONE:C_ONE + 1]
        heads = const[:, C_HEADS:C_HEADS + 2]

        def qk_parts(kind, t):
            return (a_hi[:, 4 + t], a_lo[:, 4 + t]) if kind == "q" else (k_hi[:, t], k_lo[:, t])

        def qk_whole(b, kind, t):
            if b == 1:
                return prob[:, 1, "kq".index(kind)] if t == 0 else v_sb[:, t]
            return tmpB[:, (t + (kind == "q" and b == 2)) % 2]

        def value_tiles(b):
            return v_sb[:] if b == 0 else v_sb[:, 0].rearrange("p (k e) -> p k e", e=P)

        small_in = sem("small_in")
        x_in_ready = sem("x_in_ready")
        raw_ready = [sem(f"raw_ready{s}") for s in range(SLOTS)]
        hi_ready = sem("hi_ready")
        lo_ready = sem("lo_ready")
        products = sem("products")
        half_products = sem("half_products")
        tile_free = [sem("tile_free0"), sem("tile_free1")]
        turn_done = sem("turn_done")
        turn_free = sem("turn_free")
        out_done = sem("out_done")
        out_free = sem("out_free")
        merged = sem("merged")
        columns_done = sem("columns_done")
        scores_done = sem("scores_done")
        exp_done = sem("exp_done")
        max_done = sem("max_done")
        bound_ready = sem("bound_ready")
        dsink_ready = sem("dsink_ready")
        esink_ready = sem("esink_ready")
        probs_ready = sem("probs_ready")
        out_hi = sem("out_hi")
        a_squares = sem("a_squares")
        a_scaled = sem("a_scaled")
        roped = sem("roped")
        qk_hi = sem("qk_hi")
        qk_ready = sem("qk_ready")
        rstd_ready = sem("rstd_ready")
        head_sq = sem("head_sq")
        head_summed = sem("head_summed")
        spread = sem("spread")
        sq_ready = sem("sq_ready")
        sqacc_added = sem("sqacc_added")
        scaled = sem("scaled")
        part_hi = sem("part_hi")
        part_ready = sem("part_ready")
        out_scaled = sem("out_scaled")
        x_new = sem("x_new")
        relu_ready = sem("relu_ready")
        hidden_hi = sem("hidden_hi")
        hidden_ready = sem("hidden_ready")
        c_tanh = sem("c_tanh")
        c_ready = sem("c_ready")
        c4_hi = sem("c4_hi")
        c4_ready = sem("c4_ready")
        lam_ready = sem("lam_ready")
        lam_exp = sem("lam_exp")
        tables = sem("tables")
        dve_link = sem("dve_link")
        stored = sem("stored")

        def tokens(l):
            return NTOK if l < LAYERS - 1 else NX

        def halves(n):
            return [(0, 0, NX)] if n == NX else [(0, 0, NX), (1, NX, NTOK)]

        def units(l):
            return [(t, qt) for t in range(4) for qt in range(tokens(l) // P)]

        def scratch(k):
            return (tmpA, tmpB)[k // 2 % 2][:, k % 2]

        def fill_chunks(l, b, i):
            chunks, steps = len(FILL[l, b]) * ADA_GROUP, len(units(l))
            if b == 1 and second_early(l):
                return AHEAD if i == 0 else int(i < 1 + chunks - AHEAD)
            return (i + 1) * chunks // steps - i * chunks // steps

        def tile_due(todo, i):
            return todo[i + 4][0] if 0 <= i < len(todo) - 4 and todo[i + 4][1] == 0 else None

        def a_turned_after(l):
            return 0 if tokens(l) > NX else 1

        def second_early(l):
            return tokens(l) == NX

        def heads_of(l):
            n = tokens(l)
            return [[("k", 0, NTOK), ("q", 0, n)], [("q", 1, n), ("q", 2, n), ("q", 3, n)]]

        def keys(qt):
            return (0, NTOK) if qt < NX // P else (NX, NTOK)

        def fills(b, qt):
            return [[0]] if b == 0 else [[0], [1]] if qt < NX // P else [[0, 1]]

        def turned_at(group, m, c):
            return c if len(group) == 1 else c - NX + m * NY

        SH1, SC1, GM1, SH2, SC2, GM2 = (j * KT for j in range(6))

        block = ctx.enter_context(nc.Block())

        @block.sync
        def _(sp):
            sp.dma_start(c_sb[:], c_in).then_inc(small_in, 16)
            sp.dma_start(const[:], const_in).then_inc(small_in, 16)
            sp.dma_start(vec[:], vec_in).then_inc(small_in, 16)
            for c in range(DIRECT + SLOTS):
                if c >= SLOTS:
                    sp.wait_ge(products, c - SLOTS + 1)
                sp.dma_start(raw[:, c % SLOTS], w_all[c]).then_inc(raw_ready[c % SLOTS], 16)
                if SLOTS <= c < SLOTS + KT:
                    sp.dma_start(xT[:, c - SLOTS], x_in[:, c - SLOTS]).then_inc(x_in_ready, 16)
            with sp.Fori(DIRECT // SLOTS + 1, NCHUNK // SLOTS) as r:
                for s in range(SLOTS):
                    sp.wait_ge(lo_ready, r * SLOTS + (s + 1 - SLOTS - DIRECT))
                    sp.dma_start(raw[:, s], w_all[bass.ds(r * SLOTS + s, 1)].rearrange("a p n -> p (a n)")
                                 ).then_inc(raw_ready[s], 16)
            for k in range(KT):
                sp.wait_ge(x_new, KT * (2 * LAYERS - 1) + k + 1)
                sp.dma_start(out[:, k], xT[:, k, 0:NX]).then_inc(stored, 16)
            sp.wait_ge(stored, 16 * KT)

        @block.gpsimd
        def _(pool):
            with pool.Fori(DIRECT // SLOTS, NCHUNK // SLOTS) as r:
                for s in range(SLOTS):
                    pool.wait_ge(hi_ready, r * SLOTS + (s + 1 - DIRECT))
                    nc.gpsimd.tensor_tensor(w_lo[:, s], raw[:, s], w_hi[:, s].bitcast(F32),
                                            ALU.subtract).then_inc(lo_ready, 1)

        @block.scalar
        def _(act):
            at = Place()
            def high_part(c):
                act.wait_ge(raw_ready[c % SLOTS], at.v("raw", 16 * (c // SLOTS + 1)))
                if c >= DIRECT + SLOTS:
                    act.wait_ge(products, at.v("chunk", c - SLOTS + 1))
                nc.scalar.activation(w_hi[:, c % SLOTS], raw[:, c % SLOTS], ACT.Copy).then_inc(hi_ready, 1)

            def next_chunk():
                if DIRECT <= at.chunk + AHEAD < NCHUNK:
                    high_part(at.chunk + AHEAD)
                at.chunk += 1

            def silu_c():
                act.wait_ge(small_in, 48)
                nc.scalar.activation(c_t[:], c_sb[:], ACT.Tanh, scale=0.5).then_inc(c_tanh, 1)
                act.wait_ge(c_ready, 1)
                nc.scalar.activation(c4[:, :, 0:2], c_silu[:], ACT.Copy).then_inc(c4_hi, 1)
                act.wait_ge(lam_ready, 1)
                nc.scalar.activation(lam_s[:], lam_s[:], ACT.Exp).then_inc(lam_exp, 1)

            def modulation(groups):
                for _ in range(len(groups) * ADA_GROUP):
                    next_chunk()
                at.tile += 2 * len(groups)

            def squares_of_input():
                act.wait_ge(x_in_ready, 16 * KT)
                for k in range(KT):
                    if k >= 3:
                        act.wait_ge(sqacc_added, k - 2)
                    dst = sqacc[:] if k == 0 else tmpB[:, k % 2]
                    nc.scalar.activation(dst, xT[:, k], ACT.Square).then_inc(sq_ready, 1)
                    at.square += 1
                at.sqsum += 1

            def norm_in(l, n, shift_at):
                at.out += 1
                at.turn += 1
                for k in range(KT):
                    at.scaled += 1
                    act.wait_ge(scaled, at.scaled)
                    for s, a, z in halves(n):
                        ins = nc.scalar.activation(h_hi[:, k, a:z], scratch(k)[:, a:z], ACT.Identity,
                                                   bias=ada[:, l, shift_at + k, s:s + 1])
                    ins.then_inc(part_hi, 1)
                    at.part += 1

            def turned_values(b, t):
                act.wait_ge(turn_done, at.turn + 1)
                nc.scalar.activation(value_tiles(b)[:, :, t * P:(t + 1) * P],
                                     ps[:, BANK_T].rearrange("p (k e) -> p k e", e=P),
                                     ACT.Copy).then_inc(turn_free, 1)
                at.turn += 1

            def qk_high(b, kind, t, n):
                at.roped += 1
                act.wait_ge(roped, at.roped)
                nc.scalar.activation(qk_parts(kind, t)[0][:, 0:n], qk_whole(b, kind, t)[:, 0:n],
                                     ACT.Copy).then_inc(qk_hi, 1)

            def copy_tile(b, kind, t, m):
                dst = prob[:, 0, t % 2] if kind == "v" else qk_whole(b, kind, t)[:, 0:m]
                bank = at.tile % 2
                if kind != "v" and b != 1 and at.roped:
                    act.wait_ge(qk_ready, at.roped)
                act.wait_ge(products, at.chunk)
                nc.scalar.activation(dst, ps[:, bank, 0:m], ACT.Copy).then_inc(tile_free[bank], 1)
                at.tile += 1

            def project(l, b, attention):
                n = tokens(l)
                before = None
                for kind, t in PROJ[b]:
                    next_chunk()
                    if (kind, t) == PROJ[b][-1]:
                        next(attention)
                    m = n if kind == "q" else NTOK
                    copy_tile(b, kind, t, m)
                    if before and before[0] == "v":
                        turned_values(b, before[1])
                    elif before and (kind, t) != PROJ[b][-1]:
                        qk_high(b, *before)
                    before = kind, t, m

            def project_normed(l, attention):
                first_sum = l * 3
                j = 0
                for kind, t in PROJ[1]:
                    next_chunk()
                    if (kind, t) == ("q", 2):
                        at.turn += 2
                        qk_high(1, "k", 0, NTOK)
                        qk_high(1, "q", 0, tokens(l))
                    if (kind, t) == ("q", 3):
                        turned_values(1, 0)
                        next(attention)
                    m = tokens(l) if kind == "q" else NTOK
                    copy_tile(1, kind, t, m)
                    if kind == "v":
                        continue
                    act.wait_ge(tile_free[(at.tile - 1) % 2], (at.tile - 1) // 2 + 1)
                    if j == 2:
                        act.wait_ge(head_summed, first_sum + 1)
                    if j == 3:
                        act.wait_ge(out_done, at.out + 1)
                    if j == 4:
                        act.wait_ge(head_summed, first_sum + 2)
                    nc.scalar.activation(tmpB[:, j % 2, 0:m], qk_whole(1, kind, t)[:, 0:m],
                                         ACT.Square).then_inc(head_sq, 1)
                    j += 1
                at.out += 2
                if second_early(l):
                    at.turn += 1
                    qk_high(1, "q", 1, tokens(l))

            def attend(l, b):
                todo = units(l)

                def exponentials(i):
                    t, qt = todo[i]
                    a, z = keys(qt)
                    slot = at.unit % 2
                    act.wait_ge(bound_ready, at.unit + 1)
                    for m in range(2):
                        nc.scalar.activation(prob[:, slot, m, a:z], ps[:, BANK_S + at.map % 4, a:z], ACT.Exp,
                                             bias=negm[:, slot, m:m + 1], scale=SCALE,
                                             accum_out=sums[:, slot, m:m + 1]).then_inc(exp_done, 1)
                        at.map += 1
                    if b == 2:
                        act.wait_ge(dsink_ready, at.gate + 1)
                        nc.scalar.activation(esink[:, slot], dsink[:, slot], ACT.Exp).then_inc(esink_ready, 1)
                        at.gate += 1
                    at.unit += 1

                def output(i):
                    t, qt = todo[i]
                    if b == 0:
                        act.wait_ge(out_done, at.out + 1)
                        dst = mix[:, qt, t * P:(t + 1) * P]
                        nc.scalar.activation(dst, ps[:, BANK_O, 0:P], ACT.Copy).then_inc(out_free, 1)
                        act.wait_ge(out_free, at.out + 1)
                        nc.scalar.activation(sqacc[:, 0:P], dst, ACT.Square,
                                             accum_out=ssA[:, i:i + 1]).then_inc(a_squares, 1)
                    else:
                        act.wait_ge(turn_done, at.turn + 1)
                        nc.scalar.activation(a_hi[:, t, qt * P:(qt + 1) * P], ps[:, BANK_T, 0:P],
                                             ACT.Copy).then_inc(out_hi, 1)
                        at.turn += 1
                    at.out += 1

                exponentials(0)
                yield
                for i, (t, qt) in enumerate(todo):
                    a, z = keys(qt)
                    if i + 1 < len(todo):
                        exponentials(i + 1)
                    for group in fills(b, qt):
                        if len(group) == 2:
                            a = 0
                        act.wait_ge(turn_done, at.turn + 1)
                        nc.scalar.activation(probT[:, at.item % 2, a:z], ps[:, BANK_T, a:z],
                                             ACT.Copy).then_inc(turn_free, 1)
                        at.turn += 1
                        at.item += 1
                    if b != 1 and i < 2:
                        qk_high(b, "q", 2 + i, tokens(l))
                    if b == 1 and tile_due(todo, i - 1):
                        qk_high(1, "q", tile_due(todo, i - 1), tokens(l))
                    for _ in range(fill_chunks(l, b, i)):
                        next_chunk()
                    if i >= 1:
                        output(i - 1)
                    if b == 1 and tile_due(todo, i):
                        at.turn += 1
                output(len(todo) - 1)
                at.tile += 2 * len(FILL[l, b])

            def turned_a(l):
                n = tokens(l)
                for t in range(4):
                    act.wait_ge(turn_done, at.turn + 1)
                    nc.scalar.activation(a_hi[:, t, 0:n], ps[:, BANK_S + t, 0:n], ACT.Copy,
                                         scale=gsub[:, l:l + 1]).then_inc(out_hi, 1)
                    at.turn += 1

            def merge(l, b):
                n = tokens(l)
                for pair in range(KT // 2):
                    for j in range(2):
                        next_chunk()
                        act.wait_ge(products, at.chunk)
                        nc.scalar.activation(tmpB[:, j, 0:n], ps[:, at.tile % 2, 0:n], ACT.Tanh,
                                             scale=0.5).then_inc(tile_free[at.tile % 2], 1)
                        at.tile += 1
                        if b == 0 and pair == 0 and j == a_turned_after(l):
                            turned_a(l)
                    next_chunk()
                    at.tile += 2

            def split_merged(n):
                for k in range(KT):
                    at.merged += 1
                    act.wait_ge(merged, at.merged)
                    nc.scalar.activation(h_hi[:, k, 0:n], mix[:, k, 0:n], ACT.Copy, scale=0.5).then_inc(part_hi, 1)
                    at.part += 1

            def project_out(n):
                for k in range(KT):
                    next_chunk()
                    act.wait_ge(products, at.chunk)
                    if k >= 3:
                        act.wait_ge(sqacc_added, at.sqsum * (KT - 1) + k - 2)
                    dst = sqacc[:, 0:n] if k == 0 else tmpB[:, k % 2, 0:n]
                    nc.scalar.activation(dst, ps[:, at.tile % 2, 0:n], ACT.Square).then_inc(sq_ready, 1)
                    at.tile += 1
                    at.square += 1
                at.sqsum += 1

            def norm_out(groups, next_n):
                at.out += 1
                at.turn += 1
                if next_n:
                    for k in range(KT):
                        act.wait_ge(x_new, at.x_new + k + 1)
                        if k >= 3:
                            act.wait_ge(sqacc_added, at.sqsum * (KT - 1) + k - 2)
                        dst = sqacc[:, 0:next_n] if k == 0 else tmpB[:, k % 2, 0:next_n]
                        nc.scalar.activation(dst, xT[:, k, 0:next_n], ACT.Square).then_inc(sq_ready, 1)
                        next_chunk()
                    at.square += KT
                    at.sqsum += 1
                    at.tile += 2 * len(groups)
                at.x_new += KT

            def quarter(n, last):
                for j in range(KT):
                    next_chunk()
                    bank = at.tile % 2
                    act.wait_ge(products, at.v("chunk", at.chunk))
                    nc.scalar.activation(tmpB[:, j % 2, 0:n], ps[:, bank, 0:n], ACT.Relu).then_inc(relu_ready, 1)
                    at.tile += 1
                    at.hidden += 1
                    act.wait_ge(relu_ready, at.v("hidden", at.hidden))
                    nc.scalar.activation(a_hi[:, j, 0:n], tmpB[:, j % 2, 0:n], ACT.Square).then_inc(hidden_hi, 1)
                for k in range(KT):
                    next_chunk()
                    if last:
                        act.wait_ge(tile_free[at.tile % 2], at.tile // 2 + 1)
                        if k >= 3:
                            act.wait_ge(sqacc_added, at.sqsum * (KT - 1) + k - 2)
                        dst = sqacc[:, 0:n] if k == 0 else tmpB[:, k % 2, 0:n]
                        nc.scalar.activation(dst, mix[:, k, 0:n], ACT.Square).then_inc(sq_ready, 1)
                        at.square += 1
                    at.tile += 1
                if last:
                    at.sqsum += 1

            def mlp(n):
                quarter(n, False)
                with act.Fori(0, QUARTERS - 2) as at.round:
                    quarter(n, False)
                at.rounds(QUARTERS - 2)
                quarter(n, True)

            silu_c()
            squares_of_input()
            modulation(FIRST)
            for l in range(LAYERS):
                n = tokens(l)
                norm_in(l, NTOK, SH1)
                for b in range(3):
                    attention = attend(l, b)
                    if b == 1:
                        project_normed(l, attention)
                    else:
                        project(l, b, attention)
                    finish(attention)
                    merge(l, b)
                split_merged(n)
                project_out(n)
                norm_out(MIDDLE[l], n)
                norm_in(l, n, SH2)
                mlp(n)
                norm_out(BETWEEN.get(l), NTOK if l < LAYERS - 1 else 0)

        @block.vector
        def _(dve):
            at = Place()
            links = [0]

            def link(ins):
                links[0] += 1
                ins.then_inc(dve_link, 1)
                dve.wait_ge(dve_link, links[0])

            def setup():
                dve.wait_ge(small_in, 48)
                nc.vector.tensor_copy(idb[:], ident)
                nc.vector.tensor_copy(maskb[:].rearrange("p a b -> p (a b)"),
                                      const[:, C_MASK:C_MASK + 2 * P]).then_inc(tables, 1)
                dve.wait_ge(c_tanh, 1)
                link(nc.vector.scalar_tensor_tensor(out=c_silu[:], in0=c_t[:], scalar=1.0, in1=c_sb[:],
                                                    op0=ALU.add, op1=ALU.mult))
                nc.vector.tensor_scalar(c_silu[:], c_silu[:], 0.5, None, ALU.mult).then_inc(c_ready, 1)
                dve.wait_ge(c4_hi, 1)
                nc.vector.tensor_tensor(c4[:, :, 2:4], c_silu[:], c4[:, :, 0:2].bitcast(F32),
                                        ALU.subtract).then_inc(c4_ready, 1)
                for l in range(LAYERS):
                    v = vec[:, l, V_LAM:V_LAM + 4 * HEAD].rearrange("p (a b d) -> p a b d", a=2, b=2)
                    link(nc.vector.tensor_tensor(lam_t[:], v[:, :, 0], v[:, :, 1], ALU.mult))
                    link(nc.vector.reduce_sum(lam_s[:, 2 * l:2 * l + 2], lam_t[:], AX_X))
                nc.vector.tensor_scalar(lam_s[:], lam_s[:], 1.0, None, ALU.mult).then_inc(lam_ready, 1)
                dve.wait_ge(lam_exp, 1)
                for l in range(LAYERS):
                    lam_init = 0.8 - 0.6 * math.exp(-0.3 * l)
                    link(nc.vector.tensor_tensor(nlam[:, l:l + 1], lam_s[:, 2 * l + 1:2 * l + 2],
                                                 lam_s[:, 2 * l:2 * l + 1], ALU.subtract))
                    link(nc.vector.tensor_scalar(nlam[:, l:l + 1], nlam[:, l:l + 1], -lam_init, None, ALU.add))
                    link(nc.vector.tensor_scalar(gsub[:, l:l + 1], vec[:, l, V_GSUB:V_GSUB + 1], 1.0 - lam_init,
                                                 None, ALU.mult))
                    link(nc.vector.tensor_scalar(nsink[:, l], vec[:, l, V_SINK:V_SINK + 8], -1.0, None, ALU.mult))

            def add_squares(n, k):
                dve.wait_ge(sq_ready, at.square + k + 1)
                if k > 1:
                    dve.wait_ge(sqacc_added, at.sqsum * (KT - 1) + k - 1)
                nc.vector.tensor_tensor(sqacc[:, 0:n], sqacc[:, 0:n], tmpB[:, k % 2, 0:n],
                                        ALU.add).then_inc(sqacc_added, 1)
                if k == KT - 1:
                    at.square += KT
                    at.sqsum += 1

            def rstd(src, ncol, inv, eps, frees_out):
                v, nh, y, t = (stat[:, j, 0:ncol] for j in range(4))
                ins = nc.vector.tensor_scalar(v, src, inv, eps, ALU.mult, ALU.add)
                if frees_out:
                    ins.then_inc(out_free, 1)
                    at.out += 1
                    dve.wait_ge(out_free, at.out)
                else:
                    link(ins)
                nc.vector.tensor_scalar(nh, v, -0.5, None, ALU.mult)
                link(nc.vector.tensor_scalar(t.bitcast(I32), v.bitcast(I32), 1, None, ALU.logical_shift_right))
                link(nc.vector.tensor_scalar(y.bitcast(I32), t.bitcast(I32), -1.0, float(0x5F3759DF), ALU.mult,
                                             ALU.add))
                for j in range(3):
                    link(nc.vector.tensor_tensor(t, y, y, ALU.mult))
                    link(nc.vector.tensor_tensor(t, t, nh, ALU.mult))
                    ins = nc.vector.scalar_tensor_tensor(out=y, in0=t, scalar=1.5, in1=y, op0=ALU.add, op1=ALU.mult)
                    if j < 2:
                        link(ins)
                ins.then_inc(rstd_ready, 1)
                at.rstd += 1
                dve.wait_ge(rstd_ready, at.rstd)
                return y

            def rows(g, tile):
                dve.wait_ge(products, at.chunk)
                n = 2 if at.chunk <= DIRECT else 4
                nc.vector.tensor_copy(ada_row[0:n, g % 2], ps[0:n, tile % 2]).then_inc(tile_free[tile % 2], 1)

            def columns(l, g):
                c = g * ADA_GROUP
                bank = at.tile % 2
                at.columns += 1
                dve.wait_ge(columns_done, at.columns)
                src = ps[:, bank, 0:4 * ADA_GROUP].rearrange("p (c s) -> p c s", s=4)
                dst = ada[:, l, c:c + ADA_GROUP]
                ins = nc.vector.tensor_tensor(
                    dst, src[:, :, 0:2],
                    vec[:, l, V_BADA + c:V_BADA + c + ADA_GROUP].unsqueeze(2).to_broadcast([P, ADA_GROUP, 2]),
                    ALU.add)
                if (l, g) not in FIRST:
                    link(ins)
                    ins = nc.vector.tensor_tensor(dst, dst, src[:, :, 2:4], ALU.add)
                ins.then_inc(tile_free[bank], 1)
                at.tile += 1
                if g % 2:
                    dve.wait_ge(tile_free[bank], (at.tile - 1) // 2 + 1)
                    factors(l, g)

            def factors(l, g):
                def gain(col):
                    return vec[:, l, col:col + KT].unsqueeze(2).to_broadcast([P, KT, 2])

                def pre(j, scale_at, col):
                    link(nc.vector.scalar_tensor_tensor(out=coef[:, l, j], in0=ada[:, l, scale_at:scale_at + KT],
                                                        scalar=1.0, in1=gain(col), op0=ALU.add, op1=ALU.mult))

                def post(j, gate_at, col):
                    link(nc.vector.tensor_tensor(coef[:, l, j], ada[:, l, gate_at:gate_at + KT], gain(col),
                                                 ALU.mult))

                if g == 3:
                    pre(0, SC1, V_GPRE1)
                elif g == 5:
                    post(1, GM1, V_GPOST1)
                elif g == 9:
                    pre(2, SC2, V_GPRE2)
                elif g == 11:
                    post(3, GM2, V_GPOST2)

            def modulation(groups):
                ready = None
                for l, g in groups:
                    tile = at.tile
                    at.tile += 1
                    for j in range(ADA_GROUP):
                        at.chunk += 1
                        if j == 1 and ready:
                            columns(*ready)
                        if j == ADA_GROUP - 1:
                            rows(g, tile)
                        yield
                    ready = l, g
                if ready:
                    columns(*ready)
                yield

            def token_rstd(n, steps=()):
                dve.wait_ge(out_done, at.out + 1)
                rstd(ps[:, BANK_O, 0:n // P], n // P, 1.0 / D, EPS, True)
                finish(steps)
                dve.wait_ge(turn_done, at.turn + 1)

            def norm_in(l, n, which, shift_at, steps):
                token_rstd(n, steps)

                def scale(k):
                    if k >= 4:
                        dve.wait_ge(part_ready, at.part - 1)
                    for s, a, z in halves(n):
                        ins = nc.vector.scalar_tensor_tensor(
                            out=scratch(k)[:, a:z], in0=xT[:, k, a:z], scalar=coef[:, l, which, k, s:s + 1],
                            in1=ps[:, BANK_T, a:z], op0=ALU.mult, op1=ALU.mult)
                    ins.then_inc(scaled, 1)

                def low(k):
                    dve.wait_ge(part_hi, at.part + 1)
                    for s, a, z in halves(n):
                        ins = nc.vector.scalar_tensor_tensor(
                            out=h_lo[:, k, a:z], in0=scratch(k)[:, a:z], scalar=ada[:, l, shift_at + k, s:s + 1],
                            in1=h_hi[:, k, a:z].bitcast(F32), op0=ALU.add, op1=ALU.subtract)
                    ins.then_inc(part_ready, 1)
                    at.part += 1

                for k in range(KT):
                    scale(k)
                    if k:
                        low(k - 1)
                low(KT - 1)
                at.scaled += KT
                dve.wait_ge(scaled, at.scaled)
                dve.sem_inc(turn_free, 1)
                at.turn += 1

            def norm_out(l, n, which, groups, next_n):
                token_rstd(n)
                steps = modulation(groups)

                def scale(k):
                    if k >= 2:
                        dve.wait_ge(x_new, at.x_new + k - 1)
                    for s, a, z in halves(n):
                        ins = nc.vector.scalar_tensor_tensor(
                            out=tmpA[:, k % 2, a:z], in0=mix[:, k, a:z], scalar=coef[:, l, which, k, s:s + 1],
                            in1=ps[:, BANK_T, a:z], op0=ALU.mult, op1=ALU.mult)
                    at.out_scaled += 1
                    ins.then_inc(out_scaled, 1)

                def update(k):
                    dve.wait_ge(out_scaled, at.out_scaled - (k < KT - 1))
                    nc.vector.tensor_tensor(xT[:, k, 0:n], xT[:, k, 0:n], tmpA[:, k % 2, 0:n],
                                            ALU.add).then_inc(x_new, 1)

                scale(0)
                for k in range(KT):
                    if k + 1 < KT:
                        scale(k + 1)
                    update(k)
                    if next_n:
                        if k > 1:
                            add_squares(next_n, k - 1)
                        if k == KT - 1:
                            add_squares(next_n, k)
                        next(steps)
                dve.sem_inc(turn_free, 1)
                at.turn += 1
                at.x_new += KT
                return steps

            def rope(b, kind, t):
                x = qk_whole(b, kind, t)[:, 0:NX]
                if at.roped:
                    dve.wait_ge(roped, at.roped)
                link(nc.vector.stream_shuffle(shuf[:], x, [(j + 16) % 32 for j in range(32)]))
                nc.vector.tensor_tensor(x, x, cos, ALU.mult)
                link(nc.vector.tensor_tensor(shuf[:], shuf[:], sin, ALU.mult))
                nc.vector.tensor_tensor(x, x, shuf[:], ALU.add).then_inc(roped, 1)
                at.roped += 1

            def qk_low(b, kind, t, n):
                at.qk += 1
                dve.wait_ge(qk_hi, at.qk)
                hi, lo = (part[:, 0:n] for part in qk_parts(kind, t))
                nc.vector.tensor_tensor(lo, qk_whole(b, kind, t)[:, 0:n], hi.bitcast(F32),
                                        ALU.subtract).then_inc(qk_ready, 1)

            def project(l, b, attention):
                n = tokens(l)
                at.chunk += len(PROJ[b])
                before = None
                for kind, t in PROJ[b]:
                    if (kind, t) == PROJ[b][-1]:
                        next(attention)
                    if kind == "v":
                        at.turn += 1
                    else:
                        if (kind, t) == PROJ[b][-1]:
                            break
                        dve.wait_ge(tile_free[at.tile % 2], at.tile // 2 + 1)
                        rope(b, kind, t)
                    at.tile += 1
                    if before:
                        qk_low(b, *before)
                    before = (kind, t, n if kind == "q" else NTOK) if kind != "v" else None
                at.last_tile = at.tile
                at.tile += 1

            def finish_queries(b, i, n):
                if i == 0:
                    dve.wait_ge(tile_free[at.last_tile % 2], at.last_tile // 2 + 1)
                    rope(b, "q", 3)
                qk_low(b, "q", 2 + i, n)

            def head_rstd(group):
                ncol = sum(2 * m // P for _, _, m in group)
                dve.wait_ge(out_done, at.out + 1)
                y = rstd(ps[:, BANK_O, 0:ncol], ncol, 1.0 / HEAD, EPS, True)
                parts, start = [], 0
                for _, _, m in group:
                    parts.append(y[:, start:start + 2 * m // P].rearrange("p (t h) -> p t h", h=2))
                    start += 2 * m // P
                return parts

            def expand(j, y):
                tt = y.shape[1]
                nc.vector.tensor_copy(tmpA[:, j % 2, 0:tt * P].rearrange("p (t h d) -> p t h d", t=tt, h=2),
                                      y.unsqueeze(3).to_broadcast([P, tt, 2, HEAD])).then_inc(spread, 1)

            def head_norm(l, kind, t, m):
                x = qk_whole(1, kind, t)[:, 0:m]
                col = V_GQ if kind == "q" else V_GK
                dve.wait_ge(turn_done, at.turn + 1)
                nc.vector.scalar_tensor_tensor(out=x, in0=x, scalar=vec[:, l, col:col + 1], in1=ps[:, BANK_T, 0:m],
                                               op0=ALU.mult, op1=ALU.mult).then_inc(turn_free, 1)
                at.turn += 1
                dve.wait_ge(turn_free, at.turn)
                rope(1, kind, t)

            def project_normed(l, attention):
                at.chunk += len(PROJ[1])
                at.tile += len(PROJ[1])
                groups = heads_of(l)
                for j, y in enumerate(head_rstd(groups[0])):
                    expand(j, y)
                for tile in groups[0]:
                    head_norm(l, *tile)
                for tile in groups[0]:
                    qk_low(1, *tile)
                at.turn += 1
                next(attention)
                at.query_rstd = head_rstd(groups[1]) if second_early(l) else None
                if second_early(l):
                    expand(2, at.query_rstd[0])
                    head_norm(l, *groups[1][0])
                    qk_low(1, *groups[1][0])

            def attend(l, b):
                todo = units(l)
                n = tokens(l)

                def bounds(i):
                    t, qt = todo[i]
                    a, z = keys(qt)
                    slot = at.unit % 2
                    for m in range(2):
                        dve.wait_ge(scores_done, at.map + 1)
                        nc.vector.reduce_max(mx[:, slot, m:m + 1], ps[:, BANK_S + at.map % 4, a:z],
                                             AX_X).then_inc(max_done, 1)
                        at.map += 1
                    dve.wait_ge(max_done, at.map)
                    if b == 2:
                        nc.vector.scalar_tensor_tensor(
                            out=negm[:, slot], in0=mx[:, slot], scalar=-SCALE, in1=nsink[:, l, 2 * t:2 * t + 2],
                            op0=ALU.mult, op1=ALU.min).then_inc(bound_ready, 1)
                        dve.wait_ge(bound_ready, at.unit + 1)
                        nc.vector.tensor_tensor(dsink[:, slot], negm[:, slot], nsink[:, l, 2 * t:2 * t + 2],
                                                ALU.subtract).then_inc(dsink_ready, 1)
                    else:
                        nc.vector.tensor_scalar(negm[:, slot], mx[:, slot], -SCALE, None,
                                                ALU.mult).then_inc(bound_ready, 1)
                    at.unit += 1

                def normalise(i):
                    t, qt = todo[i]
                    a, z = keys(qt)
                    slot = at.item % 2
                    dve.wait_ge(exp_done, 2 * (at.item + 1))
                    if b == 2:
                        dve.wait_ge(esink_ready, at.gate + 1)
                        at.gate += 1
                        link(nc.vector.tensor_tensor(sums[:, slot], sums[:, slot], esink[:, slot], ALU.add))
                    link(nc.vector.reciprocal(rsum[:, slot], sums[:, slot]))
                    if b == 0:
                        e = [prob[:, slot, m, a:z] for m in range(2)]
                        link(nc.vector.tensor_scalar(rsum[:, slot, 1:2], rsum[:, slot, 1:2], nlam[:, l:l + 1], None,
                                                     ALU.mult))
                        link(nc.vector.tensor_scalar(e[0], e[0], rsum[:, slot, 0:1], None, ALU.mult))
                        nc.vector.scalar_tensor_tensor(out=e[0], in0=e[1], scalar=rsum[:, slot, 1:2], in1=e[0],
                                                       op0=ALU.mult, op1=ALU.add).then_inc(probs_ready, 1)
                    at.item += 1

                def output(i):
                    slot = i % 2
                    dve.wait_ge(out_done, at.out + 1)
                    nc.vector.tensor_tensor(
                        sqacc[:, slot * P:(slot + 1) * P].rearrange("p (m d) -> p m d", m=2),
                        ps[:, BANK_O, 0:P].rearrange("p (m d) -> p m d", m=2),
                        rsum[:, (item0 + i) % 2].unsqueeze(2).to_broadcast([P, 2, HEAD]),
                        ALU.mult).then_inc(out_free, 1)
                    at.out += 1

                def output_low(i):
                    t, qt = todo[i]
                    at.split += 1
                    dve.wait_ge(out_hi, at.split)
                    cols = slice(qt * P, (qt + 1) * P)
                    nc.vector.tensor_tensor(a_lo[:, t, cols], ps[:, BANK_T, 0:P], a_hi[:, t, cols].bitcast(F32),
                                            ALU.subtract).then_inc(turn_free, 1)
                    at.turn += 1

                steps = modulation(FILL[l, b])
                item0 = at.item
                bounds(0)
                bounds(1)
                yield
                for i, (t, qt) in enumerate(todo):
                    normalise(i)
                    if i + 2 < len(todo):
                        bounds(i + 2)
                    if b == 1 and at.query_rstd is None:
                        at.query_rstd = head_rstd(heads_of(l)[1])
                    due = tile_due(todo, i) if b == 1 else None
                    if due:
                        expand(due + 1, at.query_rstd[due - 1])
                    at.turn += len(fills(b, qt))
                    if b and i >= 1:
                        output(i - 1)
                    if b != 1 and i < 2:
                        finish_queries(b, i, n)
                    if b == 1 and tile_due(todo, i - 1):
                        qk_low(1, "q", tile_due(todo, i - 1), n)
                    if b and i >= 1:
                        output_low(i - 1)
                    if due:
                        head_norm(l, "q", due, n)
                    for _ in range(fill_chunks(l, b, i)):
                        next(steps)
                if b:
                    output(len(todo) - 1)
                    output_low(len(todo) - 1)
                finish(steps)
                if b == 0:
                    at.out += len(todo)
                    at.araw += len(todo)
                    dve.wait_ge(a_squares, at.araw)
                    y = rstd(ssA[:, 0:len(todo)], len(todo), 1.0 / P, SUBLN_EPS, False)
                    for i, (t, qt) in enumerate(todo):
                        dst = mix[:, qt, t * P:(t + 1) * P]
                        nc.vector.tensor_scalar(dst, dst, y[:, i:i + 1], None, ALU.mult).then_inc(a_scaled, 1)
                    for t in range(4):
                        at.split += 1
                        dve.wait_ge(out_hi, at.split)
                        nc.vector.scalar_tensor_tensor(
                            out=a_lo[:, t, 0:n], in0=ps[:, BANK_S + t, 0:n], scalar=gsub[:, l:l + 1],
                            in1=a_hi[:, t, 0:n].bitcast(F32), op0=ALU.mult, op1=ALU.subtract).then_inc(turn_free, 1)
                        at.turn += 1

            def merge(l, b):
                n = tokens(l)
                for pair in range(KT // 2):
                    gates = at.tile
                    at.tile += 2
                    at.chunk += 3
                    for j in range(2):
                        k = 2 * pair + j
                        dve.wait_ge(tile_free[(gates + j) % 2], (gates + j) // 2 + 1)
                        if j == 0:
                            at.half += 1
                            dve.wait_ge(half_products, at.half)
                        else:
                            dve.wait_ge(products, at.chunk)
                        dst = mix[:, k, 0:n] if b == 0 else tmpA[:, j, 0:n]
                        bank = at.tile % 2
                        nc.vector.scalar_tensor_tensor(
                            out=dst, in0=tmpB[:, j, 0:n], scalar=1.0, in1=ps[:, bank, 0:n],
                            op0=ALU.add, op1=ALU.mult).then_inc(tile_free[bank], 1)
                        if b:
                            dve.wait_ge(tile_free[bank], at.tile // 2 + 1)
                            ins = nc.vector.tensor_tensor(mix[:, k, 0:n], mix[:, k, 0:n], tmpA[:, j, 0:n], ALU.add)
                            if b == 1:
                                link(ins)
                            else:
                                ins.then_inc(merged, 1)
                        at.tile += 1

            def split_merged(n):
                for k in range(KT):
                    dve.wait_ge(part_hi, at.part + 1)
                    ins = nc.vector.scalar_tensor_tensor(
                        out=h_lo[:, k, 0:n], in0=mix[:, k, 0:n], scalar=0.5, in1=h_hi[:, k, 0:n].bitcast(F32),
                        op0=ALU.mult, op1=ALU.subtract)
                    ins.then_inc(part_ready, 1)
                    at.part += 1

            def project_out(n):
                at.chunk += KT
                for k in range(KT):
                    bank = at.tile % 2
                    dve.wait_ge(sq_ready, at.square + k + 1)
                    nc.vector.tensor_copy(mix[:, k, 0:n], ps[:, bank, 0:n]).then_inc(tile_free[bank], 1)
                    at.tile += 1
                    if 1 <= k < KT - 1:
                        add_squares(n, k)
                add_squares(n, KT - 1)

            def quarter(n, first, last):
                for j in range(KT):
                    bank = at.tile % 2
                    at.hidden += 1
                    dve.wait_ge(relu_ready, at.v("hidden", at.hidden))
                    nc.vector.scalar_tensor_tensor(out=tmpA[:, j % 2, 0:n], in0=ps[:, bank, 0:n], scalar=0.0,
                                                   in1=tmpB[:, j % 2, 0:n], op0=ALU.max,
                                                   op1=ALU.mult).then_inc(tile_free[bank], 1)
                    dve.wait_ge(tile_free[bank], at.v("bank", at.tile // 2 + 1))
                    dve.wait_ge(hidden_hi, at.v("hidden", at.hidden))
                    nc.vector.tensor_tensor(a_lo[:, j, 0:n], tmpA[:, j % 2, 0:n], a_hi[:, j, 0:n].bitcast(F32),
                                            ALU.subtract).then_inc(hidden_ready, 1)
                    at.tile += 1
                at.chunk += KT
                for k in range(KT):
                    bank = at.tile % 2
                    at.chunk += 1
                    dve.wait_ge(products, at.v("chunk", at.chunk))
                    if first:
                        ins = nc.vector.tensor_copy(mix[:, k, 0:n], ps[:, bank, 0:n])
                    else:
                        ins = nc.vector.tensor_tensor(mix[:, k, 0:n], mix[:, k, 0:n], ps[:, bank, 0:n], ALU.add)
                    ins.then_inc(tile_free[bank], 1)
                    at.tile += 1
                    if last and k > 1:
                        add_squares(n, k - 1)
                if last:
                    add_squares(n, KT - 1)

            def mlp(n):
                quarter(n, True, False)
                with dve.Fori(0, QUARTERS - 2) as at.round:
                    quarter(n, False, False)
                at.rounds(QUARTERS - 2)
                quarter(n, False, True)

            setup()
            steps = modulation(FIRST)
            for _ in range(DIRECT - ADA_GROUP):
                next(steps)
            for k in range(1, KT):
                add_squares(NTOK, k)
            for l in range(LAYERS):
                n = tokens(l)
                norm_in(l, NTOK, 0, SH1, steps)
                for b in range(3):
                    attention = attend(l, b)
                    if b == 1:
                        project_normed(l, attention)
                    else:
                        project(l, b, attention)
                    finish(attention)
                    merge(l, b)
                split_merged(n)
                project_out(n)
                steps = norm_out(l, n, 1, MIDDLE[l], n)
                norm_in(l, n, 2, SH2, steps)
                mlp(n)
                steps = norm_out(l, n, 3, BETWEEN.get(l, []), NTOK if l < LAYERS - 1 else 0)

        @block.tensor
        def _(pe):
            at = Place()

            def blocks(bank, jobs, hi, lo, n, ready=None):
                slot = at.chunk % SLOTS
                for i, (blk, k) in enumerate(jobs):
                    if ready:
                        ready(k)
                    cols = slice(blk * P, (blk + 1) * P)
                    for p, (w, a) in enumerate(((w_hi, hi), (w_lo, hi), (w_hi, lo))):
                        ins = nc.tensor.matmul(ps[:, bank, 0:n], w[:, slot, cols], a[:, k, 0:n],
                                               start=(i == 0 and p == 0), stop=(i == len(jobs) - 1 and p == 2))
                return ins

            def chunk_wait():
                pe.wait_ge(lo_ready, at.v("chunk", at.chunk + 1 - DIRECT))

            def open_tile():
                bank = at.tile % 2
                if at.tile >= 2:
                    pe.wait_ge(tile_free[bank], at.v("bank", at.tile // 2))
                at.tile += 1
                return bank

            def product_pair(hi, lo, n, ready):
                banks = [open_tile(), open_tile()]
                pe.wait_ge(lo_ready, at.v("chunk", at.chunk + 2 - DIRECT))
                for k in range(KT):
                    ready(k)
                    for j, bank in enumerate(banks):
                        slot = (at.chunk + j) % SLOTS
                        cols = slice(k * P, (k + 1) * P)
                        for p, (w, a) in enumerate(((w_hi, hi), (w_lo, hi), (w_hi, lo))):
                            ins = nc.tensor.matmul(ps[:, bank, 0:n], w[:, slot, cols], a[:, k, 0:n],
                                                   start=(k == 0 and p == 0), stop=(k == KT - 1 and p == 2))
                        if k == KT - 1:
                            ins.then_inc(products, 1)
                at.chunk += 2

            def product(hi, lo, n, ready=None):
                chunk_wait()
                blocks(open_tile(), [(k, k) for k in range(KT)], hi, lo, n, ready).then_inc(products, 1)
                at.chunk += 1

            def open_turn():
                if at.turn:
                    pe.wait_ge(turn_free, at.turn)
                at.turn += 1

            def open_out():
                if at.out:
                    pe.wait_ge(out_free, at.out)
                at.out += 1

            def turn(tiles, bank=BANK_T):
                for src, col in tiles:
                    ins = nc.tensor.transpose(ps[:, bank, col:col + P], src, ident)
                ins.then_inc(turn_done, 1)

            def row_chunk(j, bank):
                slot = at.chunk % SLOTS
                if at.chunk < DIRECT:
                    pe.wait_ge(raw_ready[slot], 16 * (at.chunk // SLOTS + 1))
                    still, moving = c_silu, (raw,)
                else:
                    chunk_wait()
                    still, moving = c4, (w_hi, w_lo)
                for k in range(KT):
                    for w in moving:
                        ins = nc.tensor.matmul(ps[0:still.shape[2], bank, j * P:(j + 1) * P], still[:, k],
                                               w[:, slot, k * P:(k + 1) * P],
                                               start=(k == 0 and w is moving[0]),
                                               stop=(k == KT - 1 and w is moving[-1]))
                ins.then_inc(products, 1)
                at.chunk += 1

            def columns(g, tile):
                pe.wait_ge(tile_free[tile % 2], tile // 2 + 1)
                bank = open_tile()
                n = 2 if at.chunk <= DIRECT else 4
                for j in range(ADA_GROUP):
                    ins = nc.tensor.transpose(ps[:, bank, 4 * j:4 * j + n], ada_row[0:n, g % 2, j * P:(j + 1) * P],
                                              ident[0:n, 0:n])
                ins.then_inc(columns_done, 1)

            def modulation(groups):
                ready = None
                for _, g in groups:
                    tile = at.tile
                    bank = open_tile()
                    for j in range(ADA_GROUP):
                        row_chunk(j, bank)
                        if j == 1 and ready:
                            columns(*ready)
                        yield
                    ready = g, tile
                if ready:
                    columns(*ready)
                yield

            def token_rstd(n, beside=None):
                at.sqsum += 1
                pe.wait_ge(sqacc_added, at.sqsum * (KT - 1))
                open_out()
                for t in range(n // P):
                    ins = nc.tensor.matmul(ps[:, BANK_O, t:t + 1], sqacc[:, t * P:(t + 1) * P], ones,
                                           start=True, stop=True)
                ins.then_inc(out_done, 1)
                if beside:
                    beside()
                at.rstd += 1
                pe.wait_ge(rstd_ready, at.rstd)
                open_turn()
                turn([(stat[:, 2, t:t + 1].to_broadcast([P, P]), t * P) for t in range(n // P)])

            def norm_out_in(n, next_n, groups):
                steps = modulation(groups)

                def some(count):
                    for _ in range(count):
                        next(steps)

                token_rstd(n, lambda: some(2))
                some(len(groups) * ADA_GROUP - 2)
                token_rstd(next_n, lambda: some(1))

            def next_part(k):
                at.part += 1
                pe.wait_ge(part_ready, at.part)

            def turn_values(t, tile):
                pe.wait_ge(tile_free[tile % 2], tile // 2 + 1)
                open_turn()
                turn([(prob[:, 0, t % 2, j * P:(j + 1) * P], j * P) for j in range(NTOK // P)])

            def project(l, b, attention):
                n = tokens(l)
                before = None
                for i, (kind, t) in enumerate(PROJ[b]):
                    tile = at.tile
                    if b == 0 and i == 0:
                        product_pair(h_hi, h_lo, NTOK, next_part)
                        turn_values(t, tile)
                        continue
                    if b == 0 and i == 1:
                        tile -= 1
                    else:
                        if i == len(PROJ[b]) - 1:
                            next(attention)
                        product(h_hi, h_lo, n if kind == "q" else NTOK)
                    if before is not None:
                        turn_values(*before)
                    before = (t, tile) if kind == "v" else None

            def head_sums(column, j, m, done):
                at.hsq += 1
                pe.wait_ge(head_sq, at.hsq)
                for i in range(m // P):
                    ins = nc.tensor.matmul(ps[:, BANK_O, column + 2 * i:column + 2 * i + 2],
                                           tmpB[:, j % 2, i * P:(i + 1) * P], heads, start=True, stop=True)
                ins.then_inc(done, 1)

            def project_normed(l, attention):
                n = tokens(l)
                columns_of_q = 2 * n // P
                product(h_hi, h_lo, NTOK)
                product(h_hi, h_lo, n)
                open_out()
                head_sums(0, 0, NTOK, head_summed)
                value_tile = at.tile
                product(h_hi, h_lo, NTOK)
                head_sums(2 * NTOK // P, 1, n, out_done)
                product(h_hi, h_lo, n)
                at.rstd += 1
                pe.wait_ge(rstd_ready, at.rstd)
                spread_heads(0, NTOK)
                spread_heads(1, n)
                product(h_hi, h_lo, n)
                open_out()
                head_sums(0, 2, n, head_summed)
                turn_values(0, value_tile)
                next(attention)
                product(h_hi, h_lo, n)
                head_sums(columns_of_q, 3, n, head_summed)
                at.rstd += 1
                if second_early(l):
                    head_sums(2 * columns_of_q, 4, n, out_done)
                    for _ in range(fill_chunks(l, 1, 0)):
                        next(at.fill)
                    pe.wait_ge(rstd_ready, at.rstd)
                    spread_heads(2, n)

            def spread_heads(j, m):
                at.spread += 1
                pe.wait_ge(spread, at.spread)
                open_turn()
                turn([(tmpA[:, j % 2, i * P:(i + 1) * P], i * P) for i in range(m // P)])

            def attend(l, b):
                todo = units(l)
                qk_before = at.qk
                first_q = sum(kind == "k" for kind, _ in PROJ[b])
                at.qk += first_q + 4

                def scores(i, maps=(0, 1)):
                    t, qt = todo[i]
                    a, z = keys(qt)
                    kt = t if b == 0 else 0
                    pe.wait_ge(qk_ready, qk_before + first_q + t + 1)
                    window = b == 2 and qt < NX // P
                    for m in maps:
                        rows = slice(m * HEAD, (m + 1) * HEAD)
                        if at.map >= 4:
                            pe.wait_ge(exp_done, at.map - 3)
                        bank = BANK_S + at.map % 4
                        (qh, ql), (kh, kl) = qk_parts("q", t), qk_parts("k", kt)
                        for p, (q, k) in enumerate(((qh, kh), (ql, kh), (qh, kl))):
                            ins = nc.tensor.matmul(ps[:, bank, a:z], q[rows, qt * P:(qt + 1) * P], k[rows, a:z],
                                                   start=p == 0, stop=p == 2 and not window)
                        if window:
                            other = (1 - qt) * P
                            ins = nc.tensor.matmul(ps[:, bank, other:other + P], idb[:], maskb[:, qt],
                                                   start=False, stop=True)
                        ins.then_inc(scores_done, 1)
                        at.map += 1

                def turn_probs(i, group):
                    t, qt = todo[i]
                    a, z = keys(qt)
                    if b == 0:
                        at.diff += 1
                        pe.wait_ge(probs_ready, at.diff)
                    else:
                        pe.wait_ge(exp_done, map0 + 2 * i + group[-1] + 1)
                    open_turn()
                    turn([(prob[:, (at.unit + i) % 2, m, c:c + P], turned_at(group, m, c))
                          for m in group for c in range(a, z, P)])
                    at.item += 1
                    return at.turn - 1, (at.item - 1) % 2

                def weigh(i, group, event, slot):
                    t, qt = todo[i]
                    a, z = keys(qt)
                    pe.wait_ge(turn_free, event + 1)
                    if group[0] == 0:
                        open_out()
                    for m in group:
                        cols = slice(0, P) if b == 0 else slice(m * HEAD, (m + 1) * HEAD)
                        v_cols = slice(t * P, (t + 1) * P) if b == 0 else cols
                        for c in range(a, z, P):
                            col = turned_at(group, m, c)
                            ins = nc.tensor.matmul(ps[:, BANK_O, cols], probT[:, slot, col:col + P],
                                                   value_tiles(b)[:, c // P, v_cols], start=c == a, stop=c == z - P)
                    if group == fills(b, qt)[-1]:
                        ins.then_inc(out_done, 1)

                def turn_output(i):
                    pe.wait_ge(out_free, out0 + i + 1)
                    open_turn()
                    turn([(sqacc[:, (i % 2) * P:(i % 2 + 1) * P], 0)])

                if b == 2 and l == 0:
                    pe.wait_ge(tables, 1)
                map0 = at.map
                steps = at.fill = modulation(FILL[l, b])
                scores(0)
                scores(1)
                yield
                out0 = at.out
                before = None
                for i, (t, qt) in enumerate(todo):
                    if i + 2 < len(todo):
                        scores(i + 2, (0,))
                    if b and i >= 2:
                        turn_output(i - 2)
                    if i + 2 < len(todo):
                        scores(i + 2, (1,))
                    if b == 1 and tile_due(todo, i - 1):
                        spread_heads(tile_due(todo, i - 1) + 1, tokens(l))
                    if not (b == 1 and i == 0 and second_early(l)):
                        for _ in range(fill_chunks(l, b, i)):
                            next(steps)
                    if b == 1 and i == 0 and not second_early(l):
                        head_sums(2 * (2 * tokens(l) // P), 4, tokens(l), out_done)
                    for group in fills(b, qt):
                        event, slot = turn_probs(i, group)
                        if before:
                            weigh(*before)
                        before = (i, group, event, slot)
                if b:
                    turn_output(len(todo) - 2)
                weigh(*before)
                finish(steps)
                if b:
                    turn_output(len(todo) - 1)
                at.unit += len(todo)
                if b == 0:
                    at.rstd += 1

            def turn_a(l):
                ntt = tokens(l) // P
                for t in range(4):
                    at.scaled += ntt
                    pe.wait_ge(a_scaled, at.scaled)
                    turn([(mix[:, j, t * P:(t + 1) * P], j * P) for j in range(ntt)], BANK_S + t)
                    at.turn += 1

            def merge(l, b):
                n = tokens(l)
                for pair in range(KT // 2):
                    for j in range(2):
                        product(h_hi, h_lo, n)
                        if b == 0 and pair == 0 and j == a_turned_after(l):
                            turn_a(l)
                    if pair == 0:
                        pe.wait_ge(turn_free, at.turn)
                        pe.wait_ge(out_free, at.out)
                    chunk_wait()
                    for j in range(2):
                        blocks(open_tile(), [(4 * j + i, i) for i in range(4)], a_hi, a_lo, n
                               ).then_inc(products if j else half_products, 1)
                    at.chunk += 1

            def project_out(n):
                product_pair(h_hi, h_lo, n, next_part)
                for _ in range(2, KT):
                    product(h_hi, h_lo, n)

            def quarter(n, first):
                if first:
                    product_pair(h_hi, h_lo, n, next_part)
                for _ in range(2 if first else 0, KT):
                    product(h_hi, h_lo, n)

                def next_hidden(k):
                    at.hidden += 1
                    pe.wait_ge(hidden_ready, at.v("hidden", at.hidden))

                for k in range(KT):
                    product(a_hi, a_lo, n, next_hidden if k == 0 else None)

            def mlp(n):
                quarter(n, True)
                with pe.Fori(0, QUARTERS - 2) as at.round:
                    quarter(n, False)
                at.rounds(QUARTERS - 2)
                quarter(n, False)

            pe.wait_ge(small_in, 48)
            pe.wait_ge(c_ready, 1)
            steps = modulation(FIRST)
            for _ in range(DIRECT - 2):
                next(steps)
            token_rstd(NTOK, lambda: (next(steps), next(steps)))
            finish(steps)
            pe.wait_ge(c4_ready, 1)
            for l in range(LAYERS):
                n = tokens(l)
                for b in range(3):
                    attention = attend(l, b)
                    if b == 1:
                        project_normed(l, attention)
                    else:
                        project(l, b, attention)
                    finish(attention)
                    merge(l, b)
                project_out(n)
                norm_out_in(n, n, MIDDLE[l])
                mlp(n)
                if l < LAYERS - 1:
                    norm_out_in(n, NTOK, BETWEEN[l])
                else:
                    token_rstd(n)


def arrange(inputs):
    def blocks(w):
        return w.reshape(-1, P, P).transpose(1, 0, 2).reshape(P, -1)

    def pair_heads(a, axis):
        a = np.moveaxis(a, axis, 0)
        a = a.reshape((2, 4, HEAD) + a.shape[1:]).swapaxes(0, 1).reshape(a.shape)
        return np.moveaxis(a, 0, axis)

    chunks, vecs = [], []
    for l in range(LAYERS):
        w_in, w_branch = inputs["w_in"][l], inputs["w_branch"][l]
        w_out, w1, w2 = inputs["w_out"][l], inputs["w_ff1"][l], inputs["w_ff2"][l]
        cols = lambda w, j: w[:, j * P:(j + 1) * P]
        ada_chunks = lambda groups: [blocks(cols(inputs["w_ada"][layer], g * ADA_GROUP + j))
                                     for layer, g in groups for j in range(ADA_GROUP)]
        if l == 0:
            chunks += ada_chunks(FIRST)
        widths = dict(qa=512, ka=512, va=512, qb=512, kb=P, vb=P, qc=512, kc=P, vc=P, gt=3 * D)
        part, start = {}, 0
        for name, width in widths.items():
            part[name] = w_in[:, start:start + width]
            start += width
        for b, name in enumerate("abc"):
            if b:
                part["q" + name] = pair_heads(part["q" + name], 1)
            wb = w_branch[b * 512:(b + 1) * 512]
            if b:
                wb = pair_heads(wb, 0)
            chunks += [blocks(cols(part[kind + name], t)) for kind, t in PROJ[b]]
            chunks += ada_chunks(FILL[l, b])
            for pair in range(KT // 2):
                chunks += [blocks(cols(part["gt"], b * KT + 2 * pair + j)) for j in range(2)]
                chunks.append(np.concatenate([blocks(cols(wb, 2 * pair + j)) for j in range(2)], 1))
        chunks += [blocks(cols(w_out, j)) for j in range(KT)]
        chunks += ada_chunks(MIDDLE[l])
        for r in range(QUARTERS):
            chunks += [blocks(cols(w1, r * KT + j)) for j in range(KT)]
            chunks += [blocks(cols(w2[r * D:(r + 1) * D], j)) for j in range(KT)]
        chunks += ada_chunks(BETWEEN.get(l, []))
        v = np.zeros((P, NV), np.float32)
        v[:, V_BADA:V_BADA + ADA_CHUNKS] = inputs["b_ada"][l].reshape(-1, P).T
        for col, name in ((V_GPRE1, "g_pre_mix"), (V_GPOST1, "g_post_mix"), (V_GPRE2, "g_pre_ff"),
                          (V_GPOST2, "g_post_ff")):
            v[:, col:col + KT] = inputs[name][l].reshape(KT, P).T
        v[:, V_GQ] = np.tile(inputs["g_qnorm"][l], 2)
        v[:, V_GK] = np.tile(inputs["g_knorm"][l], 2)
        v[:, V_GSUB] = inputs["g_subln"][l]
        v[:, V_SINK:V_SINK + 8] = inputs["sink"][l].reshape(2, 4).T.reshape(1, 8)
        for j, name in enumerate(("lam_q1", "lam_k1", "lam_q2", "lam_k2")):
            v[:, V_LAM + j * HEAD:V_LAM + (j + 1) * HEAD] = inputs[name][l][None]
        vecs.append(v)
    feature_major = lambda a: a.reshape(-1, KT, P).transpose(2, 1, 0)
    x = np.concatenate([inputs["x"][0], inputs["ctx"][0]], 0)
    c = np.concatenate([inputs["c"], inputs["c_ctx"][None]], 0)
    return {
        "x_in": np.ascontiguousarray(feature_major(x)),
        "w_all": np.stack(chunks),
        "vec_in": np.ascontiguousarray(np.stack(vecs, 1)),
        "c_in": np.ascontiguousarray(feature_major(c)),
        "const_in": shape_constants(),
    }


def kernel(**inputs):
    import concourse.bacc as bacc
    from concourse.bass_utils import run_bass_kernel_spmd

    arrays = arrange({k: np.asarray(v) for k, v in inputs.items()})
    nc = bacc.Bacc("TRN2", target_bir_lowering=False, num_devices=1)
    args = [nc.dram_tensor(name, a.shape, F32, kind="ExternalInput").ap() for name, a in arrays.items()]
    args.append(nc.dram_tensor("out", (P, KT, NX), F32, kind="ExternalOutput").ap())
    build_trunk(nc, *args)
    r = run_bass_kernel_spmd(nc, [arrays], core_ids=[0])
    return r.results[0]["out"].transpose(2, 1, 0).reshape(1, NX, D)
```
